# Optimizing a Trainium2 kernel written in Bass

```python
import math
import jax, jax.numpy as jnp
from jax import lax
import numpy as np

D_MODEL = 1024
BATCH = 1
SEQ = 256
DEPTH = 1

HG_HEADS = 8
HG_DK = 128
HG_DV = D_MODEL // HG_HEADS
HG_CHUNK = 32

NSA_HEADS = 8
NSA_GROUPS = 2
NSA_REP = NSA_HEADS // NSA_GROUPS
NSA_DK = 128
NSA_DV = 128
CMP_BLOCK = 32
CMP_STRIDE = 16
CMP_HIDDEN = 128
SLC_BLOCK = 64
SLC_TOPK = 16
WINDOW = 512
Q_BLOCK = 64
FORCE_SCORE = 1e4

REL_BUCKETS = 32
REL_MAX_DIST = 128

N_GROUPS = 4
EXP_PER_GROUP = 8
N_EXPERTS = N_GROUPS * EXP_PER_GROUP
TOPK_IN_GROUP = 2
D_EXPERT = D_MODEL // 2
MOE_BLOCK = 128

ALPHA = (2 * DEPTH) ** 0.25
BETA = (8 * DEPTH) ** -0.25

SPLITS = (HG_HEADS * HG_DK, HG_HEADS * HG_DK, HG_HEADS * HG_DV, HG_HEADS * HG_DV,
          NSA_HEADS * NSA_DK,
          NSA_GROUPS * NSA_DK, NSA_GROUPS * NSA_DV,
          NSA_GROUPS * NSA_DK, NSA_GROUPS * NSA_DV,
          NSA_GROUPS * NSA_DK, NSA_GROUPS * NSA_DV,
          3 * NSA_HEADS, D_MODEL, D_MODEL)
D_IN = sum(SPLITS)


def _layer_norm(x, eps=1e-5):
    xf = x.astype(jnp.float32)
    mu = jnp.mean(xf, axis=-1, keepdims=True)
    var = jnp.mean(jnp.square(xf - mu), axis=-1, keepdims=True)
    return ((xf - mu) * lax.rsqrt(var + eps)).astype(x.dtype)

def _rms_norm(x, eps=1e-6):
    xf = x.astype(jnp.float32)
    return (xf * lax.rsqrt(jnp.mean(jnp.square(xf), axis=-1, keepdims=True) + eps)).astype(x.dtype)

def _masked_softmax(logits, mask):
    lf = jnp.where(mask, logits.astype(jnp.float32), -1e30)
    p = jax.nn.softmax(lf, axis=-1)
    return jnp.where(mask, p, 0.0)

def _rel_bucket(dist):
    n = jnp.maximum(dist, 0)
    max_exact = REL_BUCKETS // 2
    nf = jnp.maximum(n, 1).astype(jnp.float32)
    large = max_exact + (jnp.log(nf / max_exact) / math.log(REL_MAX_DIST / max_exact)
                         * (REL_BUCKETS - max_exact)).astype(jnp.int32)
    large = jnp.minimum(large, REL_BUCKETS - 1)
    return jnp.where(n < max_exact, n, large)

def _hgrn2(q, f_raw, v, lb):
    B, T = q.shape[:2]
    N = T // HG_CHUNK
    lb = lb.reshape(HG_HEADS, HG_DK).astype(q.dtype)
    f = lb + (1 - lb) * jax.nn.sigmoid(f_raw)
    log_f = jnp.log(f)
    k = 1 - f

    def chunks(a):
        return a.reshape(B, N, HG_CHUNK, HG_HEADS, a.shape[-1]).transpose(1, 0, 3, 2, 4)

    qc, kc, vc, lfc = chunks(q), chunks(k), chunks(v), chunks(log_f)
    b = jnp.cumsum(lfc, axis=3)
    b_last = b[:, :, :, -1:, :]
    q_in = qc * jnp.exp(b)
    k_in = kc * jnp.exp(-b)
    k_end = kc * jnp.exp(b_last - b)
    causal = jnp.tril(jnp.ones((HG_CHUNK, HG_CHUNK), dtype=bool))
    att = jnp.einsum('nbhid,nbhjd->nbhij', q_in, k_in)
    att = jnp.where(causal, att, 0)
    o_intra = jnp.einsum('nbhij,nbhje->nbhie', att, vc)
    upd = jnp.einsum('nbhcd,nbhce->nbhde', k_end, vc)
    decay = jnp.exp(b_last[:, :, :, 0, :])

    def step(S, xs):
        q_n, dec_n, u_n = xs
        o_n = jnp.einsum('bhcd,bhde->bhce', q_n, S)
        S = dec_n[..., None] * S + u_n
        return S, o_n

    S0 = jnp.zeros((B, HG_HEADS, HG_DK, HG_DV), q.dtype)
    _, o_inter = lax.scan(step, S0, (q_in, decay, upd))
    o = o_intra + o_inter
    return o.transpose(1, 0, 3, 2, 4).reshape(B, T, HG_HEADS, HG_DV)

def _compress(kv, pos, w1, b1, w2):
    B, G, T, d = kv.shape
    r = CMP_BLOCK // CMP_STRIDE
    ns = T // CMP_STRIDE
    sub = kv.reshape(B, G, ns, CMP_STRIDE, d)
    blocks = jnp.concatenate([sub[:, :, j:ns - r + 1 + j] for j in range(r)], axis=3)
    blocks = (blocks + pos).reshape(B, G, ns - r + 1, CMP_BLOCK * d)
    return jax.nn.silu(blocks @ w1 + b1) @ w2

def _nsa(q, kc, vc, ks, vs, kw, vw, gate_raw, rel_bias,
         pos_k, w1_k, b1_k, w2_k, pos_v, w1_v, b1_v, w2_v):
    B, T = q.shape[:2]
    G, R = NSA_GROUPS, NSA_REP
    NQB = T // Q_BLOCK
    NSLC = T // SLC_BLOCK
    NSEL = min(SLC_TOPK, NSLC)
    scale = NSA_DK ** -0.5
    to_g = lambda a: a.transpose(0, 2, 1, 3)

    k_cmp = _compress(to_g(kc), pos_k, w1_k, b1_k, w2_k)
    v_cmp = _compress(to_g(vc), pos_v, w1_v, b1_v, w2_v)
    NC = k_cmp.shape[2]
    cmp_end = jnp.arange(NC) * CMP_STRIDE + CMP_BLOCK - 1
    cs = np.arange(NC) * CMP_STRIDE
    ss = np.arange(NSLC) * SLC_BLOCK
    overlap = jnp.asarray(((cs[:, None] < ss[None, :] + SLC_BLOCK)
                           & (cs[:, None] + CMP_BLOCK > ss[None, :])).astype(np.float32))

    k_slc = to_g(ks).reshape(B, G, NSLC, SLC_BLOCK, NSA_DK)
    v_slc = to_g(vs).reshape(B, G, NSLC, SLC_BLOCK, NSA_DV)
    pad = ((0, 0), (0, 0), (WINDOW, 0), (0, 0))
    k_win = jnp.pad(to_g(kw), pad)
    v_win = jnp.pad(to_g(vw), pad)
    table = rel_bias.reshape(G, R, REL_BUCKETS)
    g_ix = jnp.arange(G)[None, :, None, None, None]
    r_ix = jnp.arange(R)[None, None, :, None, None]
    blk_start = jnp.arange(NSLC) * SLC_BLOCK
    j_ix = jnp.arange(NSLC)

    q_blocks = q.reshape(B, NQB, Q_BLOCK, G, R, NSA_DK).transpose(1, 0, 3, 4, 2, 5)
    gate_blocks = jax.nn.sigmoid(gate_raw).reshape(B, NQB, Q_BLOCK, G, R, 3).transpose(1, 0, 3, 4, 2, 5)
    gather = jax.vmap(jax.vmap(lambda blk, ix: blk[ix]))

    def block_fn(args):
        qb, q_blk, g_blk = args
        t = qb * Q_BLOCK + jnp.arange(Q_BLOCK)
        dist_c = t[:, None] - cmp_end[None, :]
        s_c = jnp.einsum('bgrqd,bgnd->bgrqn', q_blk, k_cmp) * scale + table[:, :, _rel_bucket(dist_c)]
        p_c = _masked_softmax(s_c, dist_c >= 0)
        o_c = jnp.einsum('bgrqn,bgnd->bgrqd', p_c.astype(v_cmp.dtype), v_cmp)
        imp = jnp.einsum('bgqn,nj->bgqj', p_c.sum(axis=2), overlap)
        cur = t // SLC_BLOCK
        forced = (j_ix[None, :] == 0) | (j_ix[None, :] == cur[:, None]) | (j_ix[None, :] == cur[:, None] - 1)
        valid = blk_start[None, :] <= t[:, None]
        score = jnp.where(valid, jnp.where(forced, FORCE_SCORE, imp), -1.0)
        _, idx = lax.top_k(score, NSEL)
        k_sel = gather(k_slc, idx).reshape(B, G, Q_BLOCK, NSEL * SLC_BLOCK, NSA_DK)
        v_sel = gather(v_slc, idx).reshape(B, G, Q_BLOCK, NSEL * SLC_BLOCK, NSA_DV)
        s_pos = (idx[..., None] * SLC_BLOCK + jnp.arange(SLC_BLOCK)).reshape(B, G, Q_BLOCK, NSEL * SLC_BLOCK)
        dist_s = t[None, None, :, None] - s_pos
        s_s = (jnp.einsum('bgrqd,bgqkd->bgrqk', q_blk, k_sel) * scale
               + table[g_ix, r_ix, _rel_bucket(dist_s)[:, :, None]])
        p_s = _masked_softmax(s_s, (dist_s >= 0)[:, :, None])
        o_s = jnp.einsum('bgrqk,bgqkd->bgrqd', p_s.astype(v_sel.dtype), v_sel)
        k_w = lax.dynamic_slice_in_dim(k_win, qb * Q_BLOCK, WINDOW + Q_BLOCK, axis=2)
        v_w = lax.dynamic_slice_in_dim(v_win, qb * Q_BLOCK, WINDOW + Q_BLOCK, axis=2)
        pos_w = qb * Q_BLOCK - WINDOW + jnp.arange(WINDOW + Q_BLOCK)
        dist_w = t[:, None] - pos_w[None, :]
        mask_w = (dist_w >= 0) & (dist_w < WINDOW) & (pos_w[None, :] >= 0)
        s_w = jnp.einsum('bgrqd,bgkd->bgrqk', q_blk, k_w) * scale + table[:, :, _rel_bucket(dist_w)]
        p_w = _masked_softmax(s_w, mask_w)
        o_w = jnp.einsum('bgrqk,bgkd->bgrqd', p_w.astype(v_w.dtype), v_w)
        return g_blk[..., 0:1] * o_c + g_blk[..., 1:2] * o_s + g_blk[..., 2:3] * o_w

    o = lax.map(block_fn, (jnp.arange(NQB), q_blocks, gate_blocks))
    return o.transpose(1, 0, 4, 2, 3, 5).reshape(B, T, NSA_HEADS * NSA_DV)

def _hier_moe(h, w_grp, b_grp, w_exp, b_exp, w1, w3, w2):
    B, T, D = h.shape
    x = h.reshape(-1, D)
    NT = x.shape[0]
    grp_prob = jax.nn.softmax((x @ w_grp + b_grp).astype(jnp.float32), axis=-1)
    grp_p, grp_idx = lax.top_k(grp_prob, 1)
    exp_logits = (x @ w_exp + b_exp).astype(jnp.float32).reshape(NT, N_GROUPS, EXP_PER_GROUP)
    in_grp = exp_logits[jnp.arange(NT), grp_idx[:, 0]]
    top_l, top_i = lax.top_k(in_grp, TOPK_IN_GROUP)
    comb = grp_p * jax.nn.softmax(top_l, axis=-1)
    expert = grp_idx * EXP_PER_GROUP + top_i

    A = NT * TOPK_IN_GROUP
    e_flat = expert.reshape(-1)
    tok_flat = jnp.repeat(jnp.arange(NT), TOPK_IN_GROUP)
    order = jnp.argsort(e_flat)
    e_s, tok_s, w_s = e_flat[order], tok_flat[order], comb.reshape(-1)[order]
    counts = jnp.bincount(e_flat, length=N_EXPERTS)
    starts = jnp.cumsum(counts) - counts
    padded = (counts + MOE_BLOCK - 1) // MOE_BLOCK * MOE_BLOCK
    pend = jnp.cumsum(padded)
    pstarts = pend - padded
    dest = pstarts[e_s] + jnp.arange(A) - starts[e_s]
    n_blocks = -(-A // MOE_BLOCK) + N_EXPERTS
    x_pad = jnp.zeros((n_blocks * MOE_BLOCK, D), x.dtype).at[dest].set(x[tok_s])
    block_expert = jnp.minimum(jnp.searchsorted(pend, jnp.arange(n_blocks) * MOE_BLOCK, side='right'),
                               N_EXPERTS - 1)

    def expert_block(args):
        xb, e = args
        return (jax.nn.silu(xb @ w1[e]) * (xb @ w3[e])) @ w2[e]

    y_pad = lax.map(expert_block, (x_pad.reshape(n_blocks, MOE_BLOCK, D), block_expert)).reshape(-1, D)
    y = y_pad[dest] * w_s[:, None].astype(x.dtype)
    out = jnp.zeros_like(x).at[tok_s].add(y)
    return out.reshape(B, T, D)

def first_inputs(seed: int = 0) -> dict:
    key = jax.random.key(seed)
    ks = iter(jax.random.split(key, 40))
    nrm = lambda shape, s: jax.random.normal(next(ks), shape, jnp.float32) * s
    L, D = DEPTH, D_MODEL
    return {
        'x': nrm((BATCH, SEQ, D), 1.0),
        'c': nrm((BATCH, D), 1.0),
        'ada_w': nrm((L, D, 6 * D), 0.1 * D ** -0.5),
        'ada_b': nrm((L, 6 * D), 0.02),
        'w_in': nrm((L, D, D_IN), D ** -0.5),
        'b_in': nrm((L, D_IN), 0.02),
        'hg_lb_logits': nrm((DEPTH + 1, HG_HEADS * HG_DK), 0.1),
        'hg_norm_w': 1.0 + nrm((L, HG_HEADS * HG_DV), 0.05),
        'cmp_pos_k': nrm((L, CMP_BLOCK, NSA_DK), 0.1),
        'cmp_w1_k': nrm((L, CMP_BLOCK * NSA_DK, CMP_HIDDEN), (CMP_BLOCK * NSA_DK) ** -0.5),
        'cmp_b1_k': nrm((L, CMP_HIDDEN), 0.02),
        'cmp_w2_k': nrm((L, CMP_HIDDEN, NSA_DK), CMP_HIDDEN ** -0.5),
        'cmp_pos_v': nrm((L, CMP_BLOCK, NSA_DV), 0.1),
        'cmp_w1_v': nrm((L, CMP_BLOCK * NSA_DV, CMP_HIDDEN), (CMP_BLOCK * NSA_DV) ** -0.5),
        'cmp_b1_v': nrm((L, CMP_HIDDEN), 0.02),
        'cmp_w2_v': nrm((L, CMP_HIDDEN, NSA_DV), CMP_HIDDEN ** -0.5),
        'rel_bias': nrm((NSA_HEADS, REL_BUCKETS), 0.5),
        'w_br_hg': nrm((L, HG_HEADS * HG_DV, D), BETA * (HG_HEADS * HG_DV) ** -0.5),
        'w_br_nsa': nrm((L, NSA_HEADS * NSA_DV, D), BETA * (NSA_HEADS * NSA_DV) ** -0.5),
        'w_out': nrm((L, D, D), BETA * D ** -0.5),
        'ln1_g': 1.0 + nrm((L, D), 0.05),
        'ln1_b': nrm((L, D), 0.02),
        'router_grp_w': nrm((L, D, N_GROUPS), D ** -0.5),
        'router_grp_b': nrm((L, N_GROUPS), 0.01),
        'router_exp_w': nrm((L, D, N_EXPERTS), D ** -0.5),
        'router_exp_b': nrm((L, N_EXPERTS), 0.01),
        'exp_w1': nrm((L, N_EXPERTS, D, D_EXPERT), D ** -0.5),
        'exp_w3': nrm((L, N_EXPERTS, D, D_EXPERT), D ** -0.5),
        'exp_w2': nrm((L, N_EXPERTS, D_EXPERT, D), BETA * D_EXPERT ** -0.5),
        'ln2_g': 1.0 + nrm((L, D), 0.05),
        'ln2_b': nrm((L, D), 0.02),
    }

def first_block(x, c, ada_w, ada_b, w_in, b_in, hg_lb_logits, hg_norm_w,
              cmp_pos_k, cmp_w1_k, cmp_b1_k, cmp_w2_k, cmp_pos_v, cmp_w1_v, cmp_b1_v, cmp_w2_v,
              rel_bias, w_br_hg, w_br_nsa, w_out, ln1_g, ln1_b,
              router_grp_w, router_grp_b, router_exp_w, router_exp_b,
              exp_w1, exp_w3, exp_w2, ln2_g, ln2_b):
    B, T, D = x.shape
    split_idx = [int(v) for v in np.cumsum(SPLITS)[:-1]]
    lb_all = jnp.cumsum(jax.nn.softmax(hg_lb_logits.astype(jnp.float32), axis=0), axis=0)
    c_act = jax.nn.silu(c)
    for l in range(DEPTH):
        mod = c_act @ ada_w[l] + ada_b[l]
        sh1, sc1, g1, sh2, sc2, g2 = jnp.split(mod, 6, axis=-1)

        h = _layer_norm(x) * (1 + sc1[:, None]) + sh1[:, None]
        proj = h @ w_in[l] + b_in[l]
        (hq, hf, hi, hg, nq, kc, vc, ks, vs, kw, vw, ngate, mg_h, mg_n) = jnp.split(proj, split_idx, axis=-1)
        o_h = _hgrn2(hq.reshape(B, T, HG_HEADS, HG_DK), hf.reshape(B, T, HG_HEADS, HG_DK),
                     hi.reshape(B, T, HG_HEADS, HG_DV), lb_all[l])
        o_h = (_rms_norm(o_h) * hg_norm_w[l].reshape(HG_HEADS, HG_DV)
               * jax.nn.sigmoid(hg.reshape(B, T, HG_HEADS, HG_DV))).reshape(B, T, HG_HEADS * HG_DV)
        gsz = (B, T, NSA_GROUPS, NSA_DK)
        o_n = _nsa(nq.reshape(B, T, NSA_HEADS, NSA_DK),
                   kc.reshape(gsz), vc.reshape(gsz), ks.reshape(gsz), vs.reshape(gsz),
                   kw.reshape(gsz), vw.reshape(gsz),
                   ngate.reshape(B, T, NSA_HEADS, 3), rel_bias,
                   cmp_pos_k[l], cmp_w1_k[l], cmp_b1_k[l], cmp_w2_k[l],
                   cmp_pos_v[l], cmp_w1_v[l], cmp_b1_v[l], cmp_w2_v[l])
        merged = jax.nn.sigmoid(mg_h) * (o_h @ w_br_hg[l]) + jax.nn.sigmoid(mg_n) * (o_n @ w_br_nsa[l])
        y = (1 + g1[:, None]) * (merged @ w_out[l])
        x = _layer_norm(ALPHA * x + y) * ln1_g[l] + ln1_b[l]

        h = _layer_norm(x) * (1 + sc2[:, None]) + sh2[:, None]
        y = (1 + g2[:, None]) * _hier_moe(h, router_grp_w[l], router_grp_b[l], router_exp_w[l],
                                          router_exp_b[l], exp_w1[l], exp_w3[l], exp_w2[l])
        x = _layer_norm(ALPHA * x + y) * ln2_g[l] + ln2_b[l]
    return x


N_MEM = 256
HEAD_DIM = 64
ATT_HEADS = 4
ATT_WIDTH = ATT_HEADS * HEAD_DIM
CONV_WIDTH = 384
CONV_KERNEL = 31
CONV_PAD = CONV_KERNEL // 2
RWKV_HEADS = 6
RWKV_WIDTH = RWKV_HEADS * HEAD_DIM
MIX_WIDTH = ATT_WIDTH + CONV_WIDTH + RWKV_WIDTH
DECAY_RANK = 64
ICLR_RANK = 64
GATE_RANK = 128
RWKV_PROJ = 3 * RWKV_WIDTH + 2 * DECAY_RANK + 2 * ICLR_RANK + GATE_RANK
IN_PROJ = ATT_WIDTH + 2 * CONV_WIDTH + RWKV_PROJ
N_EXPERTS_2 = 16
EXPERT_FF = 1024
CAPACITY_FACTOR = 2
NORM_EPS = 1e-6
LN_EPS = 1e-5
GN_EPS = 64e-5
L2_EPS = 1e-12
DECAY_SCALE = 0.606531


def rms_norm(x, g):
    xf = x.astype(jnp.float32)
    y = xf * lax.rsqrt(jnp.mean(xf * xf, axis=-1, keepdims=True) + NORM_EPS)
    return (y * g.astype(jnp.float32)).astype(x.dtype)

def memory_cross_attention(q, mem_n, w_mk, w_mv):
    B, S, _ = q.shape
    qh = q.reshape(B, S, ATT_HEADS, HEAD_DIM)
    kh = (mem_n @ w_mk).reshape(B, -1, ATT_HEADS, HEAD_DIM)
    vh = (mem_n @ w_mv).reshape(B, -1, ATT_HEADS, HEAD_DIM)
    s = jnp.einsum('bqhd,bmhd->bhqm', qh, kh).astype(jnp.float32) * (HEAD_DIM ** -0.5)
    pr = jax.nn.softmax(s, axis=-1).astype(vh.dtype)
    o = jnp.einsum('bhqm,bmhd->bqhd', pr, vh)
    return o.reshape(B, S, ATT_WIDTH)

def conformer_conv(pc, conv_w, conv_b, ln_g, ln_b):
    val, gate = jnp.split(pc, 2, axis=-1)
    u = val * jax.nn.sigmoid(gate)
    u = lax.conv_general_dilated(
        u, conv_w[:, None, :].astype(u.dtype), window_strides=(1,),
        padding=[(CONV_PAD, CONV_PAD)], dimension_numbers=('NWC', 'WIO', 'NWC'),
        feature_group_count=CONV_WIDTH) + conv_b.astype(u.dtype)
    uf = u.astype(jnp.float32)
    mu = jnp.mean(uf, axis=-1, keepdims=True)
    var = jnp.mean(jnp.square(uf - mu), axis=-1, keepdims=True)
    uf = (uf - mu) * lax.rsqrt(var + LN_EPS) * ln_g.astype(jnp.float32) + ln_b.astype(jnp.float32)
    return jax.nn.silu(uf).astype(pc.dtype)

def token_shift_centred(p, mu):
    prev = jnp.pad(p, ((0, 0), (1, 0), (0, 0)))[:, :-1]
    nxt = jnp.pad(p, ((0, 0), (0, 1), (0, 0)))[:, 1:]
    return p + mu[0] * (prev - p) + mu[1] * (nxt - p)

def wkv7_scan(r, w, k, v, kk, a, reverse):
    def step(state, inp):
        r_t, w_t, k_t, v_t, kk_t, a_t = inp
        sa = jnp.einsum('bhij,bhj->bhi', state, -kk_t)
        state = (state * w_t[..., None, :]
                 + sa[..., :, None] * (kk_t * a_t)[..., None, :]
                 + v_t[..., :, None] * k_t[..., None, :])
        y_t = jnp.einsum('bhij,bhj->bhi', state, r_t)
        return state, y_t
    S, B, H, N = r.shape
    state0 = jnp.zeros((B, H, N, N), jnp.float32)
    _, ys = lax.scan(step, state0, (r, w, k, v, kk, a), reverse=reverse)
    return ys

def rwkv7_bidirectional(pr, shift_mu, decay_w0, decay_up, iclr_a0, iclr_up, gate_up,
                        k_k, k_a, r_k, lnx_g, lnx_b):
    f32 = jnp.float32
    B, S, _ = pr.shape
    pf = token_shift_centred(pr.astype(f32), shift_mu.astype(f32))
    c0 = 3 * RWKV_WIDTH
    cuts = [RWKV_WIDTH, 2 * RWKV_WIDTH, c0, c0 + DECAY_RANK, c0 + 2 * DECAY_RANK,
            c0 + 2 * DECAY_RANK + ICLR_RANK, c0 + 2 * DECAY_RANK + 2 * ICLR_RANK]
    r, k, v, wdf, wdb, adf, adb, gd = jnp.split(pf, cuts, axis=-1)

    def heads(t):
        return t.reshape(t.shape[:-1] + (RWKV_HEADS, HEAD_DIM))

    def tm(t):
        return jnp.moveaxis(t, 1, 0)

    g = jax.nn.sigmoid(gd) @ gate_up.astype(f32)
    kk = heads(k * k_k.astype(f32))
    kk = kk * lax.rsqrt(jnp.sum(kk * kk, axis=-1, keepdims=True) + L2_EPS)
    r_h, v_h = heads(r), heads(v)
    r_tm, v_tm, kk_tm = tm(r_h), tm(v_h), tm(kk)
    r_k32 = r_k.astype(f32)

    outs, bonuses = [], []
    for d, (wd, ad) in enumerate(((wdf, adf), (wdb, adb))):
        w = jnp.exp(-DECAY_SCALE * jax.nn.sigmoid(
            decay_w0[d].astype(f32) + jnp.tanh(wd) @ decay_up[d].astype(f32)))
        a = jax.nn.sigmoid(iclr_a0[d].astype(f32) + ad @ iclr_up[d].astype(f32))
        k_d = heads(k * (1.0 + (a - 1.0) * k_a.astype(f32)))
        ys = wkv7_scan(r_tm, tm(heads(w)), tm(k_d), v_tm, kk_tm, tm(heads(a)), reverse=(d == 1))
        outs.append(jnp.moveaxis(ys, 0, 1))
        bonuses.append(jnp.sum(r_h * k_d * r_k32, axis=-1, keepdims=True) * v_h)
    y = outs[0] + outs[1]
    mu = jnp.mean(y, axis=-1, keepdims=True)
    var = jnp.mean(jnp.square(y - mu), axis=-1, keepdims=True)
    y = ((y - mu) * lax.rsqrt(var + GN_EPS) * lnx_g.astype(f32).reshape(RWKV_HEADS, HEAD_DIM)
         + lnx_b.astype(f32).reshape(RWKV_HEADS, HEAD_DIM))
    y = (y + bonuses[0] + bonuses[1]).reshape(B, S, RWKV_WIDTH) * g
    return y.astype(pr.dtype)

def expert_choice_ffn(h, w_router, w_gate, w_up, w_down):
    B, S, D = h.shape
    cap = CAPACITY_FACTOR * S // N_EXPERTS_2
    aff = jax.nn.softmax((h @ w_router).astype(jnp.float32), axis=-1)
    gates, idx = lax.top_k(jnp.swapaxes(aff, 1, 2), cap)
    xe = jax.vmap(lambda hb, ib: hb[ib])(h, idx)
    hid = jax.nn.silu(jnp.einsum('becd,edf->becf', xe, w_gate)) * jnp.einsum('becd,edf->becf', xe, w_up)
    ye = jnp.einsum('becf,efd->becd', hid, w_down) * gates[..., None].astype(h.dtype)
    bidx = jnp.arange(B)[:, None, None]
    return jnp.zeros_like(h).at[bidx, idx].add(ye)

def second_inputs(seed: int = 0) -> dict:
    key = jax.random.key(seed)
    ks = iter(jax.random.split(key, 40))
    L, D = DEPTH, D_MODEL

    def nrm(shape, scale):
        return scale * jax.random.normal(next(ks), shape, jnp.float32)

    return {
        "x": nrm((BATCH, SEQ, D), 1.0),
        "mem": nrm((BATCH, N_MEM, D), 1.0),
        "norm_mix_g": 1.0 + nrm((L, D), 0.05),
        "norm_mem_g": 1.0 + nrm((L, D), 0.05),
        "w_in": nrm((L, D, IN_PROJ), D ** -0.5),
        "w_mk": nrm((L, D, ATT_WIDTH), D ** -0.5),
        "w_mv": nrm((L, D, ATT_WIDTH), D ** -0.5),
        "conv_w": nrm((L, CONV_KERNEL, CONV_WIDTH), CONV_KERNEL ** -0.5),
        "conv_b": nrm((L, CONV_WIDTH), 0.01),
        "conv_ln_g": 1.0 + nrm((L, CONV_WIDTH), 0.05),
        "conv_ln_b": nrm((L, CONV_WIDTH), 0.01),
        "shift_mu": jax.random.uniform(next(ks), (L, 2, RWKV_PROJ), jnp.float32, 0.0, 0.5),
        "decay_w0": nrm((L, 2, RWKV_WIDTH), 0.5),
        "decay_up": nrm((L, 2, DECAY_RANK, RWKV_WIDTH), 0.1),
        "iclr_a0": nrm((L, 2, RWKV_WIDTH), 0.5),
        "iclr_up": nrm((L, 2, ICLR_RANK, RWKV_WIDTH), 0.1),
        "gate_up": nrm((L, GATE_RANK, RWKV_WIDTH), GATE_RANK ** -0.5),
        "k_k": 0.85 + nrm((L, RWKV_WIDTH), 0.05),
        "k_a": 1.0 + nrm((L, RWKV_WIDTH), 0.05),
        "r_k": nrm((L, RWKV_HEADS, HEAD_DIM), 0.1),
        "lnx_g": 1.0 + nrm((L, RWKV_WIDTH), 0.05),
        "lnx_b": nrm((L, RWKV_WIDTH), 0.01),
        "w_out": nrm((L, MIX_WIDTH, D), MIX_WIDTH ** -0.5),
        "norm_ffn_g": 1.0 + nrm((L, D), 0.05),
        "w_router": nrm((L, D, N_EXPERTS_2), D ** -0.5),
        "w_e_gate": nrm((L, N_EXPERTS_2, D, EXPERT_FF), D ** -0.5),
        "w_e_up": nrm((L, N_EXPERTS_2, D, EXPERT_FF), D ** -0.5),
        "w_e_down": nrm((L, N_EXPERTS_2, EXPERT_FF, D), EXPERT_FF ** -0.5),
        "final_norm_g": 1.0 + nrm((D,), 0.05),
    }

def second_block(x, mem, norm_mix_g, norm_mem_g, w_in, w_mk, w_mv, conv_w, conv_b, conv_ln_g,
              conv_ln_b, shift_mu, decay_w0, decay_up, iclr_a0, iclr_up, gate_up, k_k, k_a,
              r_k, lnx_g, lnx_b, w_out, norm_ffn_g, w_router, w_e_gate, w_e_up, w_e_down,
              final_norm_g):
    for l in range(DEPTH):
        h = rms_norm(x, norm_mix_g[l])
        p = h @ w_in[l]
        q, pc, pr = jnp.split(p, [ATT_WIDTH, ATT_WIDTH + 2 * CONV_WIDTH], axis=-1)
        mem_n = rms_norm(mem, norm_mem_g[l])
        o_att = memory_cross_attention(q, mem_n, w_mk[l], w_mv[l])
        o_conv = conformer_conv(pc, conv_w[l], conv_b[l], conv_ln_g[l], conv_ln_b[l])
        o_rwkv = rwkv7_bidirectional(pr, shift_mu[l], decay_w0[l], decay_up[l], iclr_a0[l],
                                     iclr_up[l], gate_up[l], k_k[l], k_a[l], r_k[l],
                                     lnx_g[l], lnx_b[l])
        x = x + jnp.concatenate([o_att, o_conv, o_rwkv], axis=-1) @ w_out[l]
        x = x + expert_choice_ffn(rms_norm(x, norm_ffn_g[l]), w_router[l], w_e_gate[l],
                                  w_e_up[l], w_e_down[l])
    return rms_norm(x, final_norm_g)


def setup_inputs(seed=0):
    out = dict(first_inputs(seed))
    for name, value in second_inputs(seed + 1).items():
        if name != "x":
            out[name + "_2"] = value
    return out


def reference(
    x, c, ada_w, ada_b, w_in, b_in, hg_lb_logits, hg_norm_w, cmp_pos_k, cmp_w1_k, cmp_b1_k,
    cmp_w2_k, cmp_pos_v, cmp_w1_v, cmp_b1_v, cmp_w2_v, rel_bias, w_br_hg, w_br_nsa, w_out,
    ln1_g, ln1_b, router_grp_w, router_grp_b, router_exp_w, router_exp_b, exp_w1, exp_w3,
    exp_w2, ln2_g, ln2_b, mem_2, norm_mix_g_2, norm_mem_g_2, w_in_2, w_mk_2, w_mv_2, conv_w_2,
    conv_b_2, conv_ln_g_2, conv_ln_b_2, shift_mu_2, decay_w0_2, decay_up_2, iclr_a0_2,
    iclr_up_2, gate_up_2, k_k_2, k_a_2, r_k_2, lnx_g_2, lnx_b_2, w_out_2, norm_ffn_g_2,
    w_router_2, w_e_gate_2, w_e_up_2, w_e_down_2, final_norm_g_2,
):
    x = first_block(
        x, c, ada_w, ada_b, w_in, b_in, hg_lb_logits, hg_norm_w, cmp_pos_k, cmp_w1_k, cmp_b1_k,
        cmp_w2_k, cmp_pos_v, cmp_w1_v, cmp_b1_v, cmp_w2_v, rel_bias, w_br_hg, w_br_nsa, w_out,
        ln1_g, ln1_b, router_grp_w, router_grp_b, router_exp_w, router_exp_b, exp_w1, exp_w3,
        exp_w2, ln2_g, ln2_b,
    )
    return second_block(
        x, mem_2, norm_mix_g_2, norm_mem_g_2, w_in_2, w_mk_2, w_mv_2, conv_w_2, conv_b_2,
        conv_ln_g_2, conv_ln_b_2, shift_mu_2, decay_w0_2, decay_up_2, iclr_a0_2, iclr_up_2,
        gate_up_2, k_k_2, k_a_2, r_k_2, lnx_g_2, lnx_b_2, w_out_2, norm_ffn_g_2, w_router_2,
        w_e_gate_2, w_e_up_2, w_e_down_2, final_norm_g_2,
    )


_drawn_inputs = setup_inputs


def setup_inputs(seed=0):
    import zlib

    import numpy as np

    out = dict(_drawn_inputs(seed))
    spreads = {}
    factors = {'b_in': 4.49,
     'hg_lb_logits': 2.859,
     'hg_norm_w': 3.356,
     'cmp_pos_k': 8.0,
     'cmp_w1_k': 3.097,
     'cmp_b1_k': 64.0,
     'cmp_pos_v': 7.038,
     'cmp_b1_v': 8.0,
     'router_grp_b': 8.0,
     'router_exp_b': 3.375,
     'norm_mem_g_2': 8.0,
     'conv_b_2': 25.287,
     'conv_ln_b_2': 51.697,
     'k_k_2': 43.848,
     'lnx_g_2': 13.402,
     'lnx_b_2': 64.0,
     'conv_ln_g_2': 8.0,
     'k_a_2': 2.706,
     'norm_ffn_g_2': 6.839,
     'r_k_2': 2.795}
    for name, (base, spread) in spreads.items():
        noise = np.random.default_rng([zlib.crc32(name.encode()), seed]).standard_normal(out[name].shape)
        drawn = base * np.exp(spread * noise) if base else spread * noise
        out[name] = __import__('jax').numpy.asarray(drawn.astype(out[name].dtype))
    for name, factor in factors.items():
        out[name] = (out[name] * factor).astype(out[name].dtype)
    return out
```

```python
from contextlib import ExitStack

import numpy as np
import concourse.bass as bass
from concourse import mybir

F32 = mybir.dt.float32
ALU = mybir.AluOpType
ACT = mybir.ActivationFunctionType
AX = mybir.AxisListType

P = 128
D = 1024
KC = D // P
T = 256
TT = T // P
RING = 6
TILE = 4096
ALPHA = 2.0 ** 0.25
NEG = -1e30
BANKS = 8
HEADS = 8
CHUNK = 32
NC4 = P // CHUNK
NE1, NE2, CAP = 32, 16, 32
CAP1 = 32
NBLK = 15
DECAY = 0.606531


def pack(parts):
    cols, at = {}, 0
    for k, v in parts.items():
        cols[k] = (at, v.shape[1])
        at += v.shape[1]
    return cols, np.concatenate([v.astype(np.float32) for v in parts.values()], 1)


def constants():
    t = np.arange(P)
    same = (t[:, None] // CHUNK) == (t[None, :] // CHUNK)
    return pack({
        "ident": np.eye(P),
        "upto": same & (t[:, None] <= t[None, :]),
        "scan": np.tile((np.arange(T) % CHUNK != 0), (P, 1)),
        "seen": (t[:, None] + P * np.arange(TT)[None, :]) >= 31,
        "chunk": t[:, None] // CHUNK == np.arange(NC4)[None, :],
        "mhalf": np.full((P, 1), -0.5),
        "fold": (t[:, None] % 32 == np.arange(30)[None, :]),
        "gkey": np.tile(4 - np.arange(4), (P, 1)),
        "ekey": np.tile(NE1 - np.arange(NE1), (P, 1)),
    })


def causal():
    q = np.arange(T).reshape(TT, P).T
    return np.where(q[:, :, None] >= np.arange(T)[None, None, :], 0.0, NEG).reshape(P, TT * T).astype(np.float32)


def buckets():
    n = np.maximum(255 - np.arange(2 * T), 0)
    nf = np.maximum(n, 1).astype(np.float32)
    large = 16 + (np.log(nf / np.float32(16)) / np.float32(np.log(8.0)) * np.float32(16)).astype(np.int32)
    bucket = np.where(n < 16, n, np.minimum(large, 31))
    one = np.zeros((32, 2 * T), np.float32)
    one[bucket, np.arange(2 * T)] = 1
    return one


def scan_masks():
    t = np.arange(P)
    i, j = t[:, None], t[None, :]
    same = i // CHUNK == j // CHUNK
    parts = {"bone": i // 64 == j // 64, "slot": np.tile(np.arange(CAP), (P, 1))}
    for d, late in enumerate((i > j, i < j)):
        parts[f"strictT{d}"] = same & late.T
        parts[f"uptoT{d}"] = same & (late.T | (i == j))
        for m in (1, 2, 4, 8, 16):
            pair = (i // (2 * m) == j // (2 * m)) & (i // m != j // m)
            if m == 1:
                parts[f"merge1_{d}"] = -1.0 * (pair & late)
            parts[f"mergeT{m}_{d}"] = -1.0 * (pair & late.T)
    return pack(parts)


CST, CST_A = constants()
MSK, MSK_A = scan_masks()
MSK0 = MSK["strictT0"][0]
PER_D = MSK["strictT1"][0] - MSK0
UP0 = 4

VA = dict(b=0, mg=52, l0=68, l1=76, hgn=84, nmix=92, nmem=100, nffn=108)
VB = dict(mu0=0, mu1=12, w0=24, a0=30, kk=36, ka=39, rk=42, lxg=45, lxb=48, cb=51, cg=54, cbb=57, b1k=60, b1v=61)
VROWS = (116, 62, 93, 64)
N_VEC = 23

PLAN1 = [("mod", 4), ("cols", 1), ("rel", 1), ("hT", 4), ("q", 4), ("f", 4), ("v", 4), ("g", 4), ("nq", 4),
         ("kvc", 2), ("ks", 1), ("vs", 2), ("kw", 1), ("vw", 2), ("gate", 1), ("part", 2), ("hid", 2), ("kcmp", 1), ("vcmp", 1),
         ("KT", 4), ("att", 4), ("head", 3 * HEADS), ("mg0", 2), ("OHT", 4),
         ("nsa", 6 * HEADS + 6), ("br", 8),
         ("g1", 2), ("y", 4), ("mod2", 6), ("memT", 4), ("km", 1), ("vm", 2),
         ("h2T", 4), ("route", 1), ("combT", 1), ("rankT1", 1), ("comb", 16)]
PLAN2 = [("h3T", 4), ("in2", 10), ("w0", 2), ("w1", 2), ("gg", 2), ("a0", 2), ("a1", 2),
         ("kks", 2), ("vt", 2), ("matt", 10), ("bon", 2), ("scan", 4 * 54), ("cmean", 1),
         ("gn1", 2), ("y2", 4), ("cvar", 1), ("gn2", 2), ("h4T", 4), ("aff", 1), ("affT", 1), ("rankT", 1), ("xe", 8)]


def build(nc, A, out):
    with ExitStack() as ctx:
        def sb(name, n):
            return ctx.enter_context(nc.sbuf_tensor(name, [P, n], F32))

        sems = {}

        def S(name):
            if name not in sems:
                sems[name] = ctx.enter_context(nc.semaphore(name))
            return sems[name]

        ring = sb("ring", RING * TILE)
        brow = sb("brow", 3 * 512)
        xs = sb("xs", 2048)
        hTs = sb("hTs", 2048)
        cst = sb("cst", CST_A.shape[1])
        colv = sb("colv", 512)
        AR = sb("arena", 10 * 2048)
        vv = sb("vv", 1024)
        st = sb("stats", 240)
        rbias = sb("rbias", 36)
        compact = ctx.enter_context(nc.sbuf_tensor("compact", [P, 1], mybir.dt.int32))
        ccol = sb("ccol", 24)
        ps = ctx.enter_context(nc.psum_tensor("ps", [P, BANKS * 512], F32))
        relrow = nc.dram_tensor("relrow", (HEADS, P, 2 * T), F32, kind="Internal").ap()

        def C(name, rows=P):
            a, n = CST[name]
            return cst[0:rows, a:a + n]

        def arena(i, n=1):
            return AR[:, i * 2048:(i + n) * 2048]

        def v3(ap, b):
            return ap.rearrange("p (b c) -> p b c", b=b)

        def v4(ap, b, c):
            return ap.rearrange("p (b c d) -> p b c d", b=b, c=c)

        def col(stack, i):
            return colv[:, stack * 128 + i:stack * 128 + i + 1]

        def mid(ap, n):
            return ap.unsqueeze(1).to_broadcast([ap.shape[0], n, ap.shape[1]])

        def last(ap, n):
            return ap.unsqueeze(len(ap.shape)).to_broadcast(list(ap.shape) + [n])

        plan, at = {}, 0
        for name, n in PLAN1 + PLAN2:
            plan[name] = at
            at += n

        def J(name, i=0):
            return plan[name] + i

        def bank(j, n=512, rows=P):
            return ps[0:rows, (j % BANKS) * 512:(j % BANKS) * 512 + n]

        full = [S(f"bank{b}_full") for b in range(BANKS)]
        free = [S(f"bank{b}_free") for b in range(BANKS)]

        def is_full(eng, j):
            eng.wait_ge(full[j % BANKS], j // BANKS + 1)

        def is_out(eng, j):
            eng.wait_ge(free[j % BANKS], j // BANKS + 1)

        def all_out(eng, name, n):
            for i in range(n):
                is_out(eng, J(name, i))

        def frees(ins, j):
            return ins.then_inc(free[j % BANKS], 1)

        def kxn(src, c0, n=512):
            return src[:, c0:c0 + n].rearrange("(k p) n -> p k n", p=P)

        w = []
        wi, bi = A["w_in"], A["b_in"]
        for i in range(4):
            w.append(("ada", kxn(A["ada_w"], 512 * i), (8, 512), A["ada_b"][:, 512 * i:512 * i + 512]))
        for name, c0, n, biased in (("q", 0, 2, 0), ("f", 1024, 2, 0), ("v", 2048, 2, 1), ("g", 3072, 2, 1),
                                    ("nq", 4096, 2, 0), ("kvc", 5120, 1, 0), ("kvs", 5632, 1, 1),
                                    ("kvw", 6144, 1, 1)):
            for i in range(n):
                c = c0 + 512 * i
                w.append((name, kxn(wi, c), (8, 512), bi[:, c:c + 512] if biased else None))
        w.append(("gate", kxn(wi, 6656, 24), (8, 24), bi[:, 6656:6680]))
        for s in "kv":
            w.append(("cw1", A[f"cmp_w1_{s}"].rearrange("(i d) h -> d i h", d=P), (32, 128), None))
        w.append(("cw2", None, (2, 128), None))
        for c0 in (7704, 8216, 6680, 7192):
            w.append(("mg", kxn(wi, c0), (8, 512), None))
        for s in ("w_br_hg", "w_br_nsa"):
            for i in range(2):
                w.append(("br", kxn(A[s], 512 * i), (8, 512), None))
        for i in range(4, 12):
            w.append(("ada", kxn(A["ada_w"], 512 * i), (8, 512), A["ada_b"][:, 512 * i:512 * i + 512]))
            if i == 5:
                for c in range(2):
                    w.append(("wout", kxn(A["w_out"], 512 * c), (8, 512), None))
        w.append(("mem", None, (16, 256), None))
        w.append(("router", None, (8, 36), None))
        N1 = len(w)
        w += [("moe1", None, None, None)] * (3 * NE1)
        R2 = len(w)
        for i in range(5):
            w.append(("in2", kxn(A["w_in_2"], 512 * i), (8, 512), None))
        w.append(("up2", None, (3, 384), None))
        for i in range(2):
            w.append(("wout2", kxn(A["w_out_2"], 512 * i), (8, 512), None))
        w.append(("router2", kxn(A["w_router_2"], 0, 16), (8, 16), None))
        N2 = len(w)

        def slot(n, shape):
            a, b = shape
            o = (n % RING) * TILE
            return ring[:, o:o + a * b].rearrange("p (a b) -> p a b", a=a)

        loaded = [S(f"slot{s}_loaded") for s in range(RING)]
        freed = [S(f"slot{s}_freed") for s in range(RING)]
        bloaded = [S(f"brow{s}_loaded") for s in range(3)]
        PIECES = {"cw2": 2, "router": 2, "mem": 2, "up2": 3}

        def load_count(n):
            return 16 * sum(PIECES.get(w[m][0], 1) if m < len(w) else 1 for m in range(n % RING, n + 1, RING))

        def free_count(n):
            return sum(w[m][0] != "moe1" for m in range(n % RING, n + 1, RING))

        biased = [i for i, t in enumerate(w) if t[3] is not None]

        def brow_at(n):
            m = biased.index(n)
            return m, brow[0:1, (m % 3) * 512:(m % 3) * 512 + 512]

        x = v3(xs[:], TT)
        hT = v3(hTs[:], KC)
        ident = C("ident")
        stacks = v3(arena(8)[:, 0:512], 4)
        onehot = arena(9)[0:32, 0:512]
        relsb = arena(9)[0:HEADS, 512:1024]
        cbc = v3(arena(7)[:, 0:1024], 8)
        mod1 = v3(arena(5), 2)
        xn = v3(arena(6), TT)
        Q, F, L, B, E = (v3(arena(i), HEADS) for i in range(5))
        V, G = v3(arena(5), TT), v3(arena(6), TT)
        NQ = v3(arena(8), HEADS)
        kvc = v3(arena(9)[:, 0:1024], 4)
        ks = v3(arena(9)[:, 1024:1536], 2)
        kw = v3(arena(9)[:, 1536:2048], 2)
        VV = v4(vv[:], TT, 2)
        blocks = [arena(7)[:, 0:962], arena(7)[:, 1024:1986]]
        hpart = v3(arena(9)[:, 384:640], 2)
        h1 = v3(arena(9)[:, 0:60], 2)
        kcmp = arena(9)[:, 64:94]
        vcmp = v3(arena(9)[0:NBLK, 128:384], 2)
        KE, KI, KT = F, E, v3(arena(2), TT)
        AT = arena(3).rearrange("p (u t) -> p u t", u=16)
        VM = arena(4).rearrange("p (b t c v) -> p b t c v", b=2, t=TT, c=NC4)
        SH = v4(arena(7), 2, 8)
        O = v4(arena(1), TT, HEADS)
        OHT = v3(arena(4), KC)
        neg = arena(3)[:, 0:512]
        BM = v4(arena(5, 2), HEADS, TT)
        ONT = v3(arena(2), KC)
        mgh, mgn = v3(arena(3), KC), v3(arena(7), KC)
        MT = v3(arena(0), KC)
        cbc2 = v3(arena(9)[:, 0:1024], 8)
        mod2 = v3(arena(5, 2), 4)
        lnr = v3(arena(1), 2)
        tmp = arena(4)[:, 0:512]
        h2 = v3(arena(8), TT)
        rt = arena(4)
        WB = v3(arena(0, 4), NE1)
        silu = v3(arena(4)[:, 1024:2048], 4)
        hid = v4(arena(7), 2, 4)
        lnr2 = v3(arena(8), 2)
        gates = v3(st[:, 0:48], TT)
        dec = v3(st[:, 48:112], HEADS)
        bns = v4(st[:, 112:136], TT, 2)
        mv = v3(st[:, 136:140], TT)
        rstd = st[:, 140:142]
        rel = st[0:32, 142:150]
        ss = v3(st[:, 150:166], TT)
        nmx = v4(st[:, 166:178], 2, TT)
        sums = v4(st[:, 178:190], 2, TT)
        rs = v4(st[:, 190:202], 2, TT)
        lb, omlb = ccol[:, 8:16], ccol[:, 16:24]

        def probs(h):
            return arena(0)[:, (h % 2) * 1024:(h % 2) * 1024 + 1024]

        def prob(h, t, kind):
            p, n = probs(h), P * (t + 1)
            if kind == 0:
                return p[:, 768 + NBLK * t:768 + NBLK * t + NBLK]
            o = 256 * t + (kind - 1) * n
            return p[:, o:o + n]

        def probT(h, i):
            o = (h % 2) * 1024 + i * 128
            return arena(1)[:, o:o + 128]

        def jU(h, t):
            return J("head", t if h == 0 else 2 + 3 * (h - 1) + t)

        def jO(h):
            return J("head", 3 * h + 4 if h < HEADS - 1 else 3 * h + 2)

        nsa = [("scores", 0, i) for i in range(3)]
        for h in range(HEADS):
            if h + 1 < HEADS:
                nsa += [("scores", h + 1, i) for i in range(3)]
            if h + 2 < HEADS:
                nsa.append(("gate", h + 2, 0))
            nsa += [("out", h, i) for i in range(3)]

        def jS(h, i):
            return J("nsa", nsa.index(("scores", h, i)))

        def jG(i):
            return J("mg0", i) if i < 2 else J("nsa", nsa.index(("gate", i, 0)))

        def jT(h, i):
            return J("nsa", nsa.index(("out", h, i)))

        ones_row = ident[0:1, 0:1].to_broadcast([1, P])
        def small(o, n):
            return v3(rt[:, 512 + o:512 + o + TT * n], TT)

        lg, oh4, el2, oh1, oh2, comb = (small(o, n) for o, n in ((0, 36), (72, 4), (80, 32), (144, 32), (208, 32), (272, 32)))
        rt_exp = small(336, 4)
        gmax, gkm, m1, m2, rt_d = (rt[:, 856 + 2 * i:858 + 2 * i] for i in range(5))
        combT = arena(4)[0:NE1, 0:256]
        chosen, ones1, place = (arena(9)[0:NE1, 256 * i:256 * i + 256] for i in range(3))
        rank1, most = v3(rt[:, 872:936], TT), rt[0:1, 936:937]
        onep1, gatep1 = v3(arena(7), TT), v3(arena(9), TT)
        XE1 = v3(arena(0, 4), KC)
        YE1 = arena(7)[:, 0:1024]
        part1, sum1 = arena(7)[0:64, 1024:1536], arena(7)[0:64, 1536:2048]
        sg1, hid1 = arena(6)[0:CAP1, 0:512], arena(6)[0:CAP1, 512:1024]

        def is_compact(eng):
            eng.wait_ge(S("spread_ready"), 1)
            return eng.value_load(compact[0:1, 0:1], min_val=0, max_val=1)


        def all_out_heads(eng):
            for h in range(HEADS):
                is_out(eng, jO(h))

        memn, memT = v3(arena(3), TT), v3(arena(7), KC)
        xn2 = v3(arena(6), TT)
        kmT, vm = v3(vv[:, 0:512], 2), v3(vv[:, 512:1024], 2)
        qa = v3(AR[:, 17280:17792], 2)

        def c3(o, n=256):
            return v3(AR[:, o:o + 3 * n], 3)

        PR = v3(AR[:, 8448:11544], 12)
        CA, CS = c3(11600), c3(13232)
        wide = ((N2 - 1) % RING) * TILE + 2048
        CU = ring[:, wide:wide + 3 * 286].rearrange("p (a b) -> p a b", a=3)
        PF = v3(AR[:, 0:3072], 12)
        R_, K_, V_ = PF[:, 0:3], PF[:, 3:6], PF[:, 6:9]
        KKn, GG, BON, YY = c3(3072), c3(5376), c3(6144), c3(6912)
        MIX = hT
        CV = MIX[:, 2:5, :]
        SG = [c3(3840), MIX[:, 5:8]]
        AA = [c3(4608), PF[:, 9:12]]
        KKs = c3(17792)
        TMc = AR[:, 18560:18816]
        VTOK = v3(AR[:, 7680:8448], TT)
        RIN0, PIN, KIN, KKIN, PEND, KEND = (c3(8448 + 384 * i, 128) for i in range(6))
        RINS = [RIN0, ring[:, wide + 858:wide + 1242].rearrange("p (a b) -> p a b", a=3)]
        BI, BP, TM = (c3(10752 + 384 * i, 128) for i in range(3))
        DG = v3(AR[:, 10752:11264], NC4)
        RHS = v3(AR[:, 11904:12672], 6)
        PTOK, KTOK = AR[:, 12672:13056], AR[:, 13056:13440]
        WW, UU = v3(AR[:, 13440:13824], 6), v3(AR[:, 13824:14208], 6)
        WU = AR[:, 13440:14208].rearrange("p (w a b n) -> p w a b n", w=2, a=3, b=2)

        def unit(i, par):
            o = 14208 + 768 * i + 384 * par
            return v3(AR[:, o:o + 384], 3)

        GB = AR[:, 14208:15744].rearrange("p (a c n) -> p a c n", a=3, c=NC4)
        JB = AR[:, 15744:17280].rearrange("p (a c n) -> p a c n", a=3, c=NC4)
        PM, UM, VMK = (v3(AR[:, 17280 + 512 * i:17792 + 512 * i], NC4) for i in range(3))
        HS = [v3(vv[:, 384 * i:384 * i + 384], 3) for i in range(2)]
        decc = v3(st[:, 48:60], 3)
        shift0 = st[:, 60:72]

        def msk(name, d=None, rows=P):
            a, n = MSK[name]
            if d is not None:
                a -= d * PER_D
            return brow[0:rows, a:a + n]

        half_masks = brow[:, MSK0:MSK0 + PER_D]

        xf = v3(arena(0), TT)
        onep, gatep = v3(arena(1)[:, 0:1024], TT), v3(arena(1)[:, 1024:2048], TT)
        XE = v3(arena(2, 2), KC)
        xeb = [v3(arena(4)[:, 1024 + 256 * i:1280 + 256 * i], KC) for i in range(2)]
        gateR = v4(arena(4)[:, 1536:1792], TT, 4)
        sg2, hid2 = arena(5)[0:64, 0:512], arena(5)[0:64, 512:1024]
        HT2 = arena(4)[:, 0:512]
        YE = arena(5)[:, 1024:2048]
        fg = arena(6)[:, 0:1024]
        zrow = arena(6)[0:1, 1024:1536]
        aff, rank = v3(st[:, 72:104], TT), v3(st[:, 202:234], TT)
        amax, asum = st[:, 104:106], st[:, 106:108]
        affT, work, sel = (arena(7)[0:NE2, 256 * i:256 * i + 256] for i in range(3))
        top8 = arena(7)[0:NE2, 768:776]
        mmax, msum = v3(st[:, 166:170], 2), v3(st[:, 170:174], 2)

        def mprob(h):
            return v3(AR[:, 14208 + 512 * (h % 2):14720 + 512 * (h % 2)], TT)

        def mprobT(h):
            return v3(AR[:, 15232 + 512 * (h % 2):15744 + 512 * (h % 2)], TT)

        ITS = ((0, 0), (0, 1), (1, 1), (1, 0))
        NIT = 54
        IT = dict(kk=0, pt=1, kt=2, prod=3, lev=13, bv=35, wu=36, gj=38, q=44, y0=45, rec=46)

        def jI(it, name, i=0):
            return J("scan", NIT * it + IT[name] + i)

        ATT = ("S0", "S1", "T0", "S2", "T1", "O0", "S3", "T2", "T3", "O1")

        def jM(name):
            return J("matt", ATT.index(name))

        block = ctx.enter_context(nc.Block())

        @block.sync
        def _(sp):
            sp.dma_start(x, A["x"].rearrange("(t p) d -> p t d", p=P)).then_inc(S("x_loaded"), 16)

            def plain_tile(n):
                name, src, shape, bias = w[n]
                if n >= RING and w[n - RING][0] != "moe1":
                    sp.wait_ge(freed[n % RING], free_count(n - RING))
                if n >= R2 and n < R2 + RING:
                    sp.wait_ge(S("down_done"), NE1)
                arrive = loaded[n % RING]
                dst = slot(n, shape)
                if name == "cw2":
                    for i, s in enumerate("kv"):
                        sp.dma_start(dst[:, i, :], A[f"cmp_w2_{s}"]).then_inc(arrive, 16)
                elif name == "router":
                    sp.dma_start(dst[:, :, 0:4], kxn(A["router_grp_w"], 0, 4)).then_inc(arrive, 16)
                    sp.dma_start(dst[:, :, 4:36], kxn(A["router_exp_w"], 0, 32)).then_inc(arrive, 16)
                elif name == "mem":
                    sp.dma_start(dst[:, 0:8, :], kxn(A["w_mk_2"], 0, 256)).then_inc(arrive, 16)
                    sp.dma_start(dst[:, 8:16, :], kxn(A["w_mv_2"], 0, 256)).then_inc(arrive, 16)
                elif name == "up2":
                    for i, s in enumerate(("decay_up_2", "iclr_up_2", "gate_up_2")):
                        sp.dma_start(dst[:, i, :], A[s]).then_inc(arrive, 16)
                else:
                    sp.dma_start(dst, src).then_inc(arrive, 16)
                if bias is not None:
                    m, row = brow_at(n)
                    if m >= 3:
                        o = biased[m - 3]
                        sp.wait_ge(freed[o % RING], free_count(o))
                    sp.dma_start(row[:, 0:bias.shape[1]], bias).then_inc(bloaded[m % 3], 16)

            for n in range(N1):
                plain_tile(n)

            def tile1(e, kind, at):
                src = A[("exp_w1", "exp_w3", "exp_w2")[kind]][e].rearrange("(k p) n -> p k n", p=P)
                sp.dma_start(slot(N1 + at, (8, 512) if kind < 2 else (4, 1024)), src)\
                    .then_inc(loaded[(N1 + at) % RING], 16)

            order = [(0, 0), (0, 1)]
            for e in range(1, 4):
                order += [(e, 0), (e, 1), (e - 1, 2)]
            for at, (e, kind) in enumerate(order):
                if at < RING:
                    sp.wait_ge(freed[(N1 + at) % RING], free_count(N1 + at - RING))
                else:
                    e0, kind0 = order[at - RING]
                    if kind0 < 2:
                        sp.wait_ge(S("up_full"), 4 * (e0 + 1))
                    else:
                        sp.wait_ge(S("down_done"), e0 + 1)
                tile1(e, kind, at)
            with sp.Fori(0, (NE1 - 4) // 2) as i:
                for j in range(2):
                    sp.wait_ge(S("up_full"), i * 8 + 4 * (j + 3))
                    tile1(i * 2 + (4 + j), 0, 11 + 3 * j)
                    tile1(i * 2 + (4 + j), 1, 12 + 3 * j)
                    sp.wait_ge(S("down_done"), i * 2 + (j + 2))
                    tile1(i * 2 + (3 + j), 2, 13 + 3 * j)
            sp.wait_ge(S("up_full"), 4 * (NE1 - 1))
            tile1(NE1 - 1, 2, 3 * NE1 - 1)

            for n in range(R2, N2):
                plain_tile(n)

            def tile2(e, m, at):
                name, half = (("w_e_gate_2", 0), ("w_e_up_2", 0), ("w_e_gate_2", 1), ("w_e_up_2", 1),
                              ("w_e_down_2", 0), ("w_e_down_2", 1))[m]
                src = A[name][e][half * 512:(half + 1) * 512, :].rearrange("(k p) n -> p k n", p=P)
                sp.dma_start(slot(N2 + at, (4, 1024)), src).then_inc(loaded[(N2 + at) % RING], 16)

            for m in range(6):
                sp.wait_ge(freed[(N2 + m) % RING], free_count(N2 + m - RING))
                tile2(0, m, m)
            with sp.Fori(0, (NE2 - 1) // 3) as i:
                for j in range(3):
                    for m in range(6):
                        if m < 4:
                            sp.wait_ge(S("up2_tiles"), i * 6 + (2 * j + m // 2 + 1 + UP0))
                        else:
                            sp.wait_ge(S("down2_tiles"), i * 6 + (2 * j + m - 3))
                        tile2(i * 3 + (j + 1), m, m)
            sp.wait_ge(S("out_ready"), 1)
            sp.dma_start(out.rearrange("(t p) d -> p t d", p=P), x).then_inc(S("stored"), 16)
            sp.wait_ge(S("stored"), 16)

        @block.gpsimd
        def _(pool):
            def load(dst, src, name, **how):
                nc.gpsimd.dma_start(dst, src, **how).then_inc(S(name), 16)

            load(cst[:], A["cst"], "constants_loaded")
            load(ccol[:, 0:8], A["c"].rearrange("a (k p) -> p (a k)", p=P), "c_loaded",
                 allow_slow_non_contiguous=True)

            def rows(name):
                return A[name].rearrange("a (r p) -> (a r) p", p=P)

            vectors = [(0, 0, A["b_in"][0, 0:6656].rearrange("(r p) -> r p", p=P)),
                       (0, VA["mg"], A["b_in"][0, 6680:8728].rearrange("(r p) -> r p", p=P)),
                       (0, VA["l0"], rows("hg_lb_logits")), (0, VA["hgn"], rows("hg_norm_w")),
                       (0, VA["nmix"], rows("norm_mix_g_2")), (0, VA["nmem"], rows("norm_mem_g_2")),
                       (0, VA["nffn"], rows("norm_ffn_g_2")), (1, VB["mu0"], rows("shift_mu_2")),
                       (1, VB["w0"], rows("decay_w0_2")), (1, VB["a0"], rows("iclr_a0_2")),
                       (2, 0, rows("conv_w_2")), (3, 0, A["cmp_pos_k"]), (3, 32, A["cmp_pos_v"])]
            for k, s in (("kk", "k_k_2"), ("ka", "k_a_2"), ("rk", "r_k_2"), ("lxg", "lnx_g_2"), ("lxb", "lnx_b_2"),
                         ("cb", "conv_b_2"), ("cg", "conv_ln_g_2"), ("cbb", "conv_ln_b_2"), ("b1k", "cmp_b1_k"),
                         ("b1v", "cmp_b1_v")):
                vectors.append((1, VB[k], rows(s)))
            assert len(vectors) == N_VEC
            for stack, r0, src in vectors:
                load(stacks[r0:r0 + src.shape[0], stack, :], src, "vectors_loaded")
            load(rel, A["rel_bias"].rearrange("h b -> b h"), "rel_loaded", allow_slow_non_contiguous=True)
            load(onehot, A["onehot"], "rel_loaded")
            load(rbias[:, 0:4], A["router_grp_b"][0].partition_broadcast(P), "router_bias_loaded")
            load(rbias[:, 4:36], A["router_exp_b"][0].partition_broadcast(P), "router_bias_loaded")
            asked = [0]

            def rsqrt(dst, src):
                asked[0] += 1
                pool.wait_ge(S("variance_ready"), asked[0])
                half = C("mhalf").to_broadcast([P, src.shape[1]])
                nc.gpsimd.tensor_tensor(dst, src, half, ALU.pow).then_inc(S("rstd_ready"), 1)

            rsqrt(rstd, rstd)
            is_out(pool, J("rel"))
            load(relrow, relsb.unsqueeze(1).to_broadcast([HEADS, P, 2 * T]), "rel_stored")
            pool.wait_ge(S("rel_stored"), 16)
            all_out(pool, "v", 4)
            is_full(pool, J("att", 3))
            pool.wait_ge(S("constants_loaded"), 16)
            for h in range(HEADS):
                if h >= 2:
                    is_full(pool, jU(h - 2, 1))
                for t in range(TT):
                    nc.gpsimd.tensor_tensor(VM[:, h % 2, t], mid(V[:, t, h * P:(h + 1) * P], NC4),
                                            last(C("chunk"), P), ALU.mult).then_inc(S("vm_ready"), 1)
            rsqrt(st[:, 150:166], st[:, 150:166])
            pool.wait_ge(S("heads_normed"), 1)
            for t in range(TT):
                src = bass.AP(relrow.tensor, 255 - P * t, [[2 * T - 1, P], [P * 2 * T, HEADS], [1, T]])
                load(BM[:, :, t, :], src, "bias_loaded")
            load(neg, A["causal"], "bias_loaded")
            is_full(pool, J("br", 0))
            load(lnr[:, 0, :], A["ln1_g"][0].partition_broadcast(P), "ln1_loaded")
            load(lnr[:, 1, :], A["ln1_b"][0].partition_broadcast(P), "ln1_loaded")
            pool.wait_ge(S("merged_ready"), 1)
            load(memn, A["mem_2"].rearrange("(t p) d -> p t d", p=P), "mem_loaded")
            for _ in range(3):
                rsqrt(rstd, rstd)
            is_full(pool, J("comb", 15))
            load(lnr2[:, 0, :], A["ln2_g"][0].partition_broadcast(P), "ln2_loaded")
            load(lnr2[:, 1, :], A["ln2_b"][0].partition_broadcast(P), "ln2_loaded")

            def gather1(turn, at):
                late = not isinstance(turn, int)
                if late or at > 1:
                    pool.wait_ge(S("up_full"), turn * 4 + 4 * (at - 1))
                cols = bass.ds(turn * CAP1 + CAP1 * at, CAP1) if late else slice(CAP1 * at, CAP1 * at + CAP1)
                nc.gpsimd.tensor_copy(xeb[at % 2], XE1[:, :, cols]).then_inc(S("xe1_ready"), 1)
                if late or at > 0:
                    pool.wait_ge(S("turned1"), turn + at)
                for t in range(TT):
                    ins = nc.gpsimd.tensor_copy(gateR[:, t], mid(gatep1[:, t, cols], 4))
                ins.then_inc(S("gate1_ready"), 1)

            fits = is_compact(pool)
            with pool.If(fits > 0):
                all_out(pool, "comb", 16)
                gather1(0, 0)
                gather1(0, 1)
                with pool.Fori(0, (NE1 - 2) // 2) as i:
                    gather1(i * 2, 2)
                    gather1(i * 2, 3)
            rsqrt(rstd, rstd)

            pool.wait_ge(S("down_done"), NE1)
            load(brow[:, 0:MSK0 + PER_D], A["masks"][:, 0:MSK0 + PER_D], "masks_loaded")
            rsqrt(rstd, rstd)
            ptt, pts = nc.gpsimd.tensor_tensor, nc.gpsimd.tensor_scalar
            for it, (d, t) in enumerate(ITS):
                if it == 2:
                    is_full(pool, jI(1, "rec", 7))
                    pool.wait_ge(S("masks_used"), 1)
                    load(half_masks, A["masks"][:, MSK0 + PER_D:MSK0 + 2 * PER_D], "masks_loaded")
                    pool.wait_ge(S("masks_loaded"), 32)
                if it == 0:
                    pool.wait_ge(S("masks_loaded"), 16)
                for lev, m in enumerate((1, 2, 4, 8, 16)):
                    for par in range(2):
                        if lev == 0:
                            pool.wait_ge(S("at_ready"), 2 * it + par + 1)
                        elif lev >= 2:
                            is_full(pool, jI(it, "lev", 6 * (lev - 2) + par))
                        elif lev == 1:
                            pool.wait_ge(S("xt_first"), 2 * it + par + 1)
                        ptt(unit(5, par), unit(4, par), mid(msk(f"mergeT{m}_{d}", d), 3), ALU.mult)\
                            .then_inc(S("aot_ready"), 1)
                        if lev == 0:
                            pool.wait_ge(S("aot_ready"), 10 * it + par + 1)
                            ptt(unit(1, par), unit(5, par), mid(ident, 3), ALU.add).then_inc(S("xt_first"), 1)
                for pc in range(3):
                    if pc:
                        is_full(pool, jI(it, "gj", 2 * pc - 2))
                    else:
                        is_full(pool, jI(it, "lev", 18 + 1))
                        is_out(pool, jI(it, "pt"))
                    ptt(PM, mid(PTOK[:, pc * P:(pc + 1) * P], NC4), last(C("chunk"), P), ALU.mult)\
                        .then_inc(S("pm_ready"), 1)
            rsqrt(rstd, rstd)
            is_full(pool, J("xe", 7))
            load(fg, A["final_norm_g_2"][0].partition_broadcast(P), "fg_loaded")
            all_out(pool, "xe", 8)
            with pool.Fori(0, NE2 // 4) as i:
                for j in range(4):
                    pool.wait_ge(S("up2_tiles"), i * 8 + (2 * j + 2))
                    nc.gpsimd.tensor_copy(xeb[j % 2], XE[:, :, bass.ds(i * 128 + 32 * j, 32)])\
                        .then_inc(S("xe_ready"), 1)
                    pool.wait_ge(S("turned2"), i * 4 + (j + 1))
                    for t in range(TT):
                        ins = nc.gpsimd.tensor_copy(gateR[:, t], mid(gatep[:, t, bass.ds(i * 128 + 32 * j, 32)], 4))
                    ins.then_inc(S("gate_ready"), 1)
            rsqrt(rstd, rstd)

        @block.scalar
        def _(act):
            act_n = [0]

            def link(ins):
                act_n[0] += 1
                ins.then_inc(S("act_step"), 1)
                act.wait_ge(S("act_step"), act_n[0])

            def ident_bias(dst, src, bias):
                return nc.scalar.activation(dst, src, ACT.Identity, bias=bias)

            act.wait_ge(S("c_loaded"), 16)
            nc.scalar.activation(ccol[:, 0:8], ccol[:, 0:8], ACT.Silu).then_inc(S("c_silu"), 1)
            is_full(act, J("cols"))
            for i, r in enumerate(VROWS):
                ins = nc.scalar.copy(colv[:, i * 128:i * 128 + r], bank(J("cols"))[:, i * 128:i * 128 + r])
            frees(ins, J("cols"))
            is_out(act, J("cols"))
            is_full(act, J("rel"))
            frees(nc.scalar.copy(relsb, bank(J("rel"), rows=HEADS)), J("rel"))
            act.wait_ge(S("lb_logit"), 1)
            nc.scalar.activation(lb, lb, ACT.Sigmoid).then_inc(S("lb_sigmoid"), 1)
            for j in range(4):
                is_full(act, J("hT", j))
                frees(nc.scalar.copy(hT[:, 2 * j:2 * j + 2, :], v3(bank(J("hT", j)), 2)), J("hT", j))

            def pair(job, j, dst, func, stack_col):
                is_full(act, job)
                for i in range(2):
                    ins = nc.scalar.activation(dst[:, 2 * j + i, :], v3(bank(job), 2)[:, i, :], func,
                                               bias=col(0, stack_col + 2 * j + i))
                frees(ins, job)

            def chunks(name, j, dst, func, stack_col):
                pair(J(name, j), j, dst, func, stack_col)

            act.wait_ge(S("h_ready"), 1)
            for j in range(4):
                chunks("q", j, Q, ACT.Identity, 0)
            for j in range(4):
                chunks("f", j, F, ACT.Sigmoid, 8)
            for i in range(4):
                is_full(act, J("g", i))
                frees(nc.scalar.activation(G[:, i % 2, (i // 2) * 512:(i // 2) * 512 + 512], bank(J("g", i)),
                                           ACT.Sigmoid), J("g", i))
            act.wait_ge(S("f_ready"), 1)
            nc.scalar.activation(L[:], F[:], ACT.Ln).then_inc(S("log_ready"), 1)
            for j in range(4):
                chunks("nq", j, NQ, ACT.Identity, 32)
            act.wait_ge(S("rel_stored"), 16)
            for j in range(2):
                chunks("kvc", j, kvc, ACT.Identity, 40)
            act.wait_ge(S("cumsum_ready"), 1)
            nc.scalar.activation(E[:], B[:], ACT.Exp, scale=-1.0).then_inc(S("exp_ready"), 1)
            nc.scalar.activation(L[:], B[:], ACT.Exp).then_inc(S("exp_ready"), 1)
            chunks("ks", 0, ks, ACT.Identity, 44)
            for t in range(TT):
                is_full(act, J("vs", t))
                frees(nc.scalar.copy(VV[:, t, 0, :], bank(J("vs", t), 256)), J("vs", t))
            chunks("kw", 0, kw, ACT.Identity, 48)
            for t in range(TT):
                is_full(act, J("vw", t))
                frees(nc.scalar.copy(VV[:, t, 1, :], bank(J("vw", t), 256)), J("vw", t))
            is_full(act, J("gate"))
            frees(nc.scalar.activation(gates, v3(bank(J("gate"), 48), TT), ACT.Sigmoid), J("gate"))
            for i in range(2):
                is_full(act, J("part", i))
                if i == 0:
                    is_full(act, J("part", 1))
                frees(nc.scalar.copy(hpart[:, i, :], bank(J("part", i), P)), J("part", i))
            for i in range(2):
                is_full(act, J("hid", i))
                frees(nc.scalar.activation(h1[:, i, :], bank(J("hid", i), 30), ACT.Silu, bias=col(1, VB["b1k"] + i)),
                      J("hid", i))
            is_full(act, J("kcmp"))
            frees(nc.scalar.copy(kcmp, bank(J("kcmp"), 30)), J("kcmp"))
            is_full(act, J("vcmp"))
            frees(nc.scalar.copy(vcmp, v3(bank(J("vcmp"), 256, NBLK), 2)), J("vcmp"))

            for j in range(4):
                is_full(act, J("KT", j))
                if j == 0:
                    act.wait_ge(S("ke_ready"), 1)
                for t in range(TT):
                    ins = nc.scalar.copy(KT[:, t, 2 * j * P:(2 * j + 2) * P].rearrange("p (h n) -> p h n", h=2),
                                         v4(bank(J("KT", j)), 2, 2)[:, :, t, :])
                frees(ins, J("KT", j))
            for h in range(HEADS):
                is_full(act, jO(h))
                for t in range(TT):
                    ins = nc.scalar.activation(O[:, t, h, :], bank(jO(h))[:, t * P:(t + 1) * P], ACT.Square,
                                               accum_out=ss[:, t, h:h + 1])
                link(ins)
                ins = nc.scalar.copy(O[:, :, h, :], v3(bank(jO(h), 256), TT))
                frees(ins, jO(h))
            def gate_pair(i):
                dst, at = (mgn, 8) if i < 4 else (mgh, 0)
                pair(jG(i), i % 4, dst, ACT.Sigmoid, VA["mg"] + at)

            gate_pair(0)
            gate_pair(1)
            for j in range(4):
                is_full(act, J("OHT", j))
                for i in range(2):
                    ins = nc.scalar.activation(OHT[:, 2 * j + i, :], v3(bank(J("OHT", j)), 2)[:, i, :], ACT.Copy,
                                               scale=col(0, VA["hgn"] + 2 * j + i))
                frees(ins, J("OHT", j))

            def exps(h):
                act.wait_ge(S("scores_ready"), h + 1)
                for t in range(TT):
                    for kind in range(3):
                        p = prob(h, t, kind)
                        ins = nc.scalar.activation(p, p, ACT.Exp, bias=nmx[:, h % 2, t, kind:kind + 1],
                                                   accum_out=sums[:, h % 2, t, kind:kind + 1])
                ins.then_inc(S("exps_ready"), 1)

            def carry(h):
                j = jT(h, 0)
                is_full(act, j)
                nc.scalar.copy(arena(1)[:, (h % 2) * 1024:(h % 2) * 1024 + 256], bank(j, 256))
                frees(nc.scalar.copy(arena(1)[0:NBLK, (h % 2) * 1024 + 256:(h % 2) * 1024 + 512],
                                     ps[0:NBLK, (j % BANKS) * 512 + 256:(j % BANKS) * 512 + 512]), j)
                j = jT(h, 1)
                is_full(act, j)
                frees(nc.scalar.copy(arena(1)[:, (h % 2) * 1024 + 512:(h % 2) * 1024 + 1024], bank(j)), j)
                j = jT(h, 2)
                is_full(act, j)
                frees(nc.scalar.copy(ONT[:, h, :], bank(j, 256)), j)

            exps(0)
            for h in range(HEADS):
                if h + 1 < HEADS:
                    exps(h + 1)
                if h + 2 < HEADS:
                    gate_pair(h + 2)
                carry(h)
            for i in range(8):
                j = J("g1", i) if i < 2 else J("mod2", i - 2)
                is_full(act, j)
                frees(nc.scalar.copy(mod2[:, i // 2, (i % 2) * 512:(i % 2) * 512 + 512], bank(j)), j)
            for j in range(4):
                is_full(act, J("memT", j))
                for i in range(2):
                    ins = nc.scalar.activation(memT[:, 2 * j + i, :], v3(bank(J("memT", j)), 2)[:, i, :], ACT.Copy,
                                               scale=col(0, VA["nmem"] + 2 * j + i))
                frees(ins, J("memT", j))
            is_full(act, J("km"))
            frees(nc.scalar.copy(kmT, v3(bank(J("km")), 2)), J("km"))
            for t in range(TT):
                is_full(act, J("vm", t))
                frees(nc.scalar.copy(vm[:, t, :], bank(J("vm", t), 256)), J("vm", t))
            for j in range(4):
                is_full(act, J("h2T", j))
                frees(nc.scalar.copy(hT[:, 2 * j:2 * j + 2, :], v3(bank(J("h2T", j)), 2)), J("h2T", j))
            act.wait_ge(S("route_max"), 1)
            nc.scalar.activation(rt_exp, rt_exp, ACT.Exp).then_inc(S("route_exp"), 1)
            act.wait_ge(S("route_top"), 1)
            nc.scalar.activation(rt_d, rt_d, ACT.Exp).then_inc(S("route_exp"), 1)
            is_full(act, J("combT"))
            frees(nc.scalar.copy(combT, bank(J("combT"), T, NE1)), J("combT"))
            for i in range(16):
                is_full(act, J("comb", i))
                frees(nc.scalar.copy(WB[:, 2 * i:2 * i + 2, :], v3(bank(J("comb", i)), 2)), J("comb", i))

            def silus(turn, at):
                for f in range(4):
                    act.wait_ge(S("up_full"), turn * 4 + (4 * at + f + 1))
                    if not isinstance(turn, int) or at > 0:
                        act.wait_ge(S("hid_ready"), turn * 4 + (4 * (at - 1) + f + 1))
                    nc.scalar.activation(silu[:, f, :], ps[:, f * 512:f * 512 + 256], ACT.Silu)\
                        .then_inc(S("silu_ready"), 1)

            fits = is_compact(act)
            with act.If(fits > 0):
                with act.Fori(0, NE1 // 2) as i:
                    for m in range(2):
                        act.wait_ge(S("sum1_ready"), i * 2 + (m + 1))
                        nc.scalar.activation(sg1, sum1[0:32], ACT.Silu).then_inc(S("silu1_ready"), 1)
                        act.wait_ge(S("turned1"), i * 2 + (m + 1))
                        nc.scalar.copy(HT2, ps[:, m * 512:m * 512 + 512]).then_inc(S("hidT1_ready"), 1)
                        act.wait_ge(S("down1_full"), i * 2 + (m + 1))
                        nc.scalar.copy(YE1[:, 0:512], ps[:, 1024:1536]).then_inc(S("ye10_ready"), 1)
            with act.If(fits < 1):
                silus(0, 0)
                with act.Fori(0, NE1 - 1) as i:
                    silus(i, 1)

            for j in range(4):
                is_full(act, J("h3T", j))
                for i in range(2):
                    ins = nc.scalar.activation(hT[:, 2 * j + i, :], v3(bank(J("h3T", j)), 2)[:, i, :], ACT.Copy,
                                               scale=col(0, VA["nmix"] + 2 * j + i))
                frees(ins, J("h3T", j))
            act.wait_ge(S("pads_ready"), 1)
            for j in range(10):
                is_full(act, J("in2", j))
                b = v3(bank(J("in2", j)), 2)
                if j == 0:
                    ins = nc.scalar.copy(qa, b)
                elif j == 1:
                    ins = nc.scalar.copy(CA[:, 0:2, :], b)
                elif j == 2:
                    nc.scalar.copy(CA[:, 2, :], b[:, 0, :])
                    ins = nc.scalar.activation(CS[:, 0, :], b[:, 1, :], ACT.Sigmoid)
                elif j == 3:
                    ins = nc.scalar.activation(CS[:, 1:3, :], b, ACT.Sigmoid)
                else:
                    ins = nc.scalar.copy(PR[:, 2 * j - 8:2 * j - 6, 1:257], b)
                frees(ins, J("in2", j))

            act.wait_ge(S("shifted"), 1)
            nc.scalar.activation(PF[:, 9, :], PF[:, 9, :], ACT.Tanh).then_inc(S("tanh_ready"), 1)
            nc.scalar.activation(PF[:, 11, :], PF[:, 11, :], ACT.Sigmoid).then_inc(S("tanh_ready"), 1)

            def low_rank(name, dst, func, stack_col):
                for i in range(2):
                    j = J(name, i)
                    is_full(act, j)
                    for c in range(2 * i, min(3, 2 * i + 2)):
                        o = bank(j)[:, (c % 2) * 256:(c % 2) * 256 + 256]
                        if func is None:
                            ins = nc.scalar.copy(dst[:, c, :], o)
                        else:
                            ins = nc.scalar.activation(dst[:, c, :], o, func, bias=col(1, stack_col + c))
                    frees(ins, j)

            low_rank("w0", SG[0], ACT.Sigmoid, VB["w0"])
            low_rank("w1", SG[1], ACT.Sigmoid, VB["w0"] + 3)
            low_rank("gg", GG, None, None)
            low_rank("a0", AA[0], ACT.Sigmoid, VB["a0"])
            is_full(act, J("a1", 1))
            low_rank("a1", AA[1], ACT.Sigmoid, VB["a0"] + 3)
            for i in range(2):
                n = 2 - i
                act.wait_ge(S("kk_sums"), i + 1)
                dst = KKs[:, 2 * i:2 * i + n, :]
                nc.scalar.activation(dst, dst, ACT.Sqrt).then_inc(S("kk_roots"), 1)

            for t in range(TT):
                is_full(act, J("vt", t))
                frees(nc.scalar.copy(VTOK[:, t, :], bank(J("vt", t), 384)), J("vt", t))

            def decays(it):
                act.wait_ge(S("decays_ready"), it + 1)
                nc.scalar.activation(KKIN, BP, ACT.Exp, scale=-DECAY)
                nc.scalar.activation(RINS[it % 2], BI, ACT.Exp, scale=-DECAY)
                nc.scalar.activation(KIN, BI, ACT.Exp, scale=DECAY)
                nc.scalar.activation(decc, decc, ACT.Exp, scale=-DECAY).then_inc(S("decay_exps"), 1)

            def mexp(h):
                act.wait_ge(S("mem_scores"), h + 1)
                for t in range(TT):
                    ins = nc.scalar.activation(mprob(h)[:, t, :], mprob(h)[:, t, :], ACT.Exp,
                                               bias=mmax[:, h % 2, t:t + 1], accum_out=msum[:, h % 2, t:t + 1])
                ins.then_inc(S("mem_exps"), 1)

            def mcarry(h):
                is_full(act, jM(f"T{h}"))
                frees(nc.scalar.copy(mprobT(h), v3(bank(jM(f"T{h}")), TT)), jM(f"T{h}"))

            def mout(i):
                is_full(act, jM(f"O{i}"))
                frees(nc.scalar.copy(MIX[:, i, :], bank(jM(f"O{i}"), 256)), jM(f"O{i}"))

            mexp(0)
            mexp(1)
            mcarry(0)
            mexp(2)
            mcarry(1)
            mout(0)
            mexp(3)
            decays(0)
            mcarry(2)
            mcarry(3)
            mout(1)
            for it, (d, t) in enumerate(ITS):
                if it:
                    decays(it)
                j = jI(it, "kk")
                is_full(act, j)
                frees(nc.scalar.copy(RHS[:, :, 0:64], v3(bank(j, 384), 6)), j)
                for name, dst in (("pt", PTOK), ("kt", KTOK)):
                    j = jI(it, name)
                    is_full(act, j)
                    frees(nc.scalar.copy(dst, bank(j, 384)), j)
                for lev in range(4):
                    for par in range(2):
                        j = jI(it, "lev", 6 * lev + par)
                        is_full(act, j)
                        frees(nc.scalar.copy(unit(2, par), v3(bank(j, 384), 3)), j)
                j = jI(it, "bv")
                is_full(act, j)
                frees(nc.scalar.copy(RHS[:, :, 64:128], v3(bank(j, 384), 6)), j)
                for par in range(2):
                    j = jI(it, "wu", par)
                    is_full(act, j)
                    frees(nc.scalar.activation(WU[:, :, :, par, :],
                                               v4(bank(j, 384), 3, 2).rearrange("p a w n -> p w a n"), ACT.Copy,
                                               scale=-1.0), j)
                for par in range(2):
                    is_out(act, jI(it, "wu", par))
                for pc in range(3):
                    if pc:
                        is_full(act, jI(it, "gj", 2 * pc - 1))
                    for c in range(NC4):
                        ins = nc.scalar.activation(UM[:, c, :].rearrange("p (a n) -> p a n", a=2),
                                                   UU[:, 2 * pc:2 * pc + 2, :], ACT.Copy, scale=C("chunk")[:, c:c + 1])
                    ins.then_inc(S("um_ready"), 1)
            act.wait_ge(S("conv_var"), 1)
            nc.scalar.activation(CS[:, 0, :], CS[:, 0, :], ACT.Sqrt).then_inc(S("conv_root"), 1)
            act.wait_ge(S("gn_var"), 1)
            nc.scalar.activation(c3(3072), c3(3072), ACT.Sqrt).then_inc(S("gn_root"), 1)
            act.wait_ge(S("conv_normed"), 1)
            for c in range(3):
                ins = nc.scalar.activation(MIX[:, 2 + c, :], CV[:, c, :], ACT.Silu, bias=col(1, VB["cbb"] + c),
                                           scale=col(1, VB["cg"] + c))
            ins.then_inc(S("conv_ready"), 1)
            for j in range(4):
                is_full(act, J("h4T", j))
                for i in range(2):
                    ins = nc.scalar.activation(hT[:, 2 * j + i, :], v3(bank(J("h4T", j)), 2)[:, i, :], ACT.Copy,
                                               scale=col(0, VA["nffn"] + 2 * j + i))
                frees(ins, J("h4T", j))
            act.wait_ge(S("aff_max"), 1)
            nc.scalar.activation(aff, aff, ACT.Exp).then_inc(S("aff_exp"), 1)
            is_full(act, J("affT"))
            frees(nc.scalar.copy(work, bank(J("affT"), T, NE2)), J("affT"))
            for k in range(KC):
                is_full(act, J("xe", k))
                frees(nc.scalar.activation(XE[:, k, :], bank(J("xe", k)), ACT.Copy, scale=col(0, VA["nffn"] + k)),
                      J("xe", k))
            with act.Fori(0, NE2 // 4) as i:
                for j in range(4):
                    act.wait_ge(S("up2_tiles"), i * 8 + (2 * j + 2 + UP0))
                    nc.scalar.activation(sg2, ps[0:64, (j % 2) * 512:(j % 2) * 512 + 512], ACT.Silu)\
                        .then_inc(S("silu2_ready"), 1)
                    act.wait_ge(S("turned2"), i * 4 + (j + 2))
                    nc.scalar.copy(HT2, ps[:, (j % 2) * 512:(j % 2) * 512 + 512]).then_inc(S("hidT_ready"), 1)
                    act.wait_ge(S("down2_tiles"), i * 8 + (2 * j + 2))
                    nc.scalar.copy(YE[:, 0:512], ps[:, 1024:1536]).then_inc(S("ye0_ready"), 1)

        @block.tensor
        def _(pe):
            turn = [0]

            def job(name, i=0):
                return start(J(name, i))

            def start(j):
                assert j == turn[0], (j, turn[0], plan)
                turn[0] += 1
                if j >= BANKS:
                    pe.wait_ge(free[j % BANKS], j // BANKS)
                return j

            def fills(ins, j):
                ins.then_inc(full[j % BANKS], 1)

            wpos = [0]

            def tile(name):
                n = wpos[0]
                wpos[0] += 1
                assert w[n][0] == name, (w[n][0], name)
                pe.wait_ge(loaded[n % RING], load_count(n))
                if w[n][3] is not None:
                    m = biased.index(n)
                    pe.wait_ge(bloaded[m % 3], 16 * (m // 3 + 1))
                return n

            def done_with(n):
                pe.wait_ge(full[(turn[0] - 1) % BANKS], (turn[0] - 1) // BANKS + 1)
                pe.sem_inc(freed[n % RING], 1)

            def mm(o, lhsT, rhs, start=True, stop=True):
                return nc.tensor.matmul(o, lhsT, rhs, start=start, stop=stop)

            def chunk_pair(name, i, wt, c0, src):
                products(job(name, i), wt, c0, src)

            def products(j, wt, c0, src):
                for c in range(2):
                    for k in range(KC):
                        ins = mm(bank(j)[:, c * 256:c * 256 + 256], wt[:, k, c0 + c * P:c0 + (c + 1) * P],
                                 src[:, k, :], k == 0, k == KC - 1)
                fills(ins, j)

            def token_half(name, i, wt, c0, n, src, t, bias=None, o=None, j=None):
                j = job(name, i) if j is None else j
                o = bank(j, n) if o is None else o
                if bias is not None:
                    mm(o, ones_row, bias, True, False)
                for k in range(KC):
                    ins = mm(o, src[:, k, t * P:(t + 1) * P], wt[:, k, c0:c0 + n], bias is None and k == 0, k == KC - 1)
                return ins, j

            def transposes(name, src):
                for j in range(4):
                    b = job(name, j)
                    for c in range(2):
                        for t in range(TT):
                            k = 2 * j + c
                            ins = nc.tensor.transpose(bank(b)[:, c * 256 + t * P:c * 256 + (t + 1) * P],
                                                      src[:, t, k * P:(k + 1) * P], ident)
                    fills(ins, b)

            pe.wait_ge(S("constants_loaded"), 16)
            pe.wait_ge(S("cbc_ready"), 1)

            def modulation(name, i, c):
                n = tile("ada")
                j = job(name, i)
                mm(bank(j), ones_row, brow_at(n)[1], True, False)
                for k in range(KC):
                    ins = mm(bank(j), c[:, k, :], slot(n, (8, 512))[:, k, :], False, k == KC - 1)
                fills(ins, j)
                done_with(n)

            for i in range(4):
                modulation("mod", i, cbc)
            pe.wait_ge(S("vectors_loaded"), 16 * N_VEC)
            j = job("cols")
            for i, r in enumerate(VROWS):
                ins = nc.tensor.transpose(bank(j)[:, i * P:i * P + r], stacks[0:r, i, :], ident[0:r, 0:r])
            fills(ins, j)
            pe.wait_ge(S("rel_loaded"), 32)
            j = job("rel")
            fills(mm(bank(j, rows=HEADS), rel, onehot), j)
            pe.wait_ge(S("h_ready"), 1)
            transposes("hT", xn)
            all_out(pe, "hT", 4)
            for name in ("q", "f"):
                for i in range(2):
                    n = tile(name)
                    for c in range(2):
                        chunk_pair(name, 2 * i + c, slot(n, (8, 512)), 256 * c, hT)
                    done_with(n)
            for name in ("v", "g"):
                for i in range(2):
                    n = tile(name)
                    for t in range(TT):
                        ins, j = token_half(name, 2 * i + t, slot(n, (8, 512)), 0, 512, hT, t, brow_at(n)[1])
                        fills(ins, j)
                    done_with(n)
            for i in range(2):
                n = tile("nq")
                for c in range(2):
                    chunk_pair("nq", 2 * i + c, slot(n, (8, 512)), 256 * c, hT)
                done_with(n)
            n = tile("kvc")
            for c in range(2):
                chunk_pair("kvc", c, slot(n, (8, 512)), 256 * c, hT)
            done_with(n)
            for s in "sw":
                n = tile("kv" + s)
                chunk_pair("k" + s, 0, slot(n, (8, 512)), 0, hT)
                for t in range(TT):
                    ins, j = token_half("v" + s, t, slot(n, (8, 512)), 256, 256, hT, t, brow_at(n)[1][:, 256:512])
                    fills(ins, j)
                done_with(n)
            n = tile("gate")
            j = job("gate")
            for t in range(TT):
                ins, _ = token_half("gate", 0, slot(n, (8, 24)), 0, 24, hT, t, brow_at(n)[1][:, 0:24],
                                    bank(j)[:, 24 * t:24 * t + 24], j)
            fills(ins, j)
            done_with(n)
            for i in range(2):
                n = tile("cw1")
                pe.wait_ge(S("blocks_ready"), i + 1)
                j = job("part", i)
                for p in range(32):
                    q = p % 4
                    ins = mm(bank(j, P)[32 * q:32 * q + 32, :], blocks[i][:, 30 * p:30 * p + 32],
                             slot(n, (32, 128))[:, p, :], p < 4, p >= 28)
                fills(ins, j)
                done_with(n)
            for i in range(2):
                is_out(pe, J("part", i))
                j = job("hid", i)
                fills(mm(bank(j, 30), hpart[:, i, :], C("fold")), j)
            n = tile("cw2")
            is_out(pe, J("hid", 0))
            j = job("kcmp")
            fills(mm(bank(j, 30), slot(n, (2, 128))[:, 0, :], h1[:, 0, :]), j)
            is_out(pe, J("hid", 1))
            j = job("vcmp")
            for g in range(2):
                ins = mm(bank(j, rows=NBLK)[:, g * P:(g + 1) * P], h1[:, 1, g * NBLK:(g + 1) * NBLK],
                         slot(n, (2, 128))[:, 1, :])
            fills(ins, j)
            done_with(n)

            pe.wait_ge(S("ke_ready"), 1)
            for jj in range(4):
                j = job("KT", jj)
                for c in range(2):
                    for t in range(TT):
                        ins = nc.tensor.transpose(v4(bank(j), 2, 2)[:, c, t, :],
                                                  KE[:, 2 * jj + c, t * P:(t + 1) * P], ident)
                fills(ins, j)
            for jj in range(4):
                j = job("att", jj)
                for c in range(2):
                    for t in range(TT):
                        h = 2 * jj + c
                        ins = mm(v4(bank(j), 2, 2)[:, c, t, :], KI[:, h, t * P:(t + 1) * P], Q[:, h, t * P:(t + 1) * P])
                fills(ins, j)

            def updates(h):
                pe.wait_ge(S("vm_ready"), 2 * (h + 1))
                if h == 0:
                    all_out(pe, "KT", 4)
                for t in range(TT):
                    j = start(jU(h, t))
                    fills(mm(bank(j), KT[:, t, h * P:(h + 1) * P], VM[:, h % 2, t].rearrange("p c v -> p (c v)")), j)

            def outputs(h):
                is_out(pe, J("att", h // 2))
                pe.wait_ge(S("states_ready"), h + 1)
                j = start(jO(h))
                for t in range(TT):
                    o = v3(bank(j, 256), TT)[:, t, :]
                    first = 1 if t == 0 else 0
                    nc.tensor.matmul(o, AT[:, 2 * h + t, :], V[:, t, h * P:(h + 1) * P], start=True, stop=True,
                                     skip_group_check=True)
                    for c in range(first, NC4):
                        a = t * P + c * CHUNK
                        ins = nc.tensor.matmul(o[c * CHUNK:(c + 1) * CHUNK, :], Q[:, h, a:a + CHUNK],
                                               SH[:, h % 2, NC4 * t + c, :], start=False, stop=True,
                                               skip_group_check=True)
                fills(ins, j)

            updates(0)
            for h in range(HEADS):
                if h + 1 < HEADS:
                    updates(h + 1)
                outputs(h)
            n = tile("mg")
            for i in range(2):
                products(start(jG(i)), slot(n, (8, 512)), 256 * i, hT)
            done_with(n)
            pe.wait_ge(S("heads_normed"), 1)
            transposes("OHT", O.rearrange("p t h v -> p t (h v)"))

            def scores(h):
                g = h // 4
                j = start(jS(h, 0))
                for t in range(TT):
                    ins = mm(bank(j)[:, NBLK * t:NBLK * t + NBLK], NQ[:, h, t * P:(t + 1) * P],
                             kcmp[:, g * NBLK:(g + 1) * NBLK])
                fills(ins, j)
                for t in range(TT):
                    j = start(jS(h, 1 + t))
                    n = P * (t + 1)
                    for i, k in enumerate((ks, kw)):
                        ins = mm(bank(j)[:, i * n:(i + 1) * n], NQ[:, h, t * P:(t + 1) * P], k[:, g, 0:n])
                    fills(ins, j)

            def weigh(h):
                g = h // 4
                pe.wait_ge(S("probs_ready"), h + 1)
                j = start(jT(h, 0))
                for i, p in enumerate((prob(h, 0, 1), prob(h, 0, 2), prob(h, 0, 0), prob(h, 1, 0))):
                    n = p.shape[1]
                    ins = nc.tensor.transpose(bank(j, rows=n)[:, i * P:(i + 1) * P], p, ident)
                fills(ins, j)
                j = start(jT(h, 1))
                for i in range(4):
                    p = prob(h, 1, 1 + i // 2)[:, (i % 2) * P:(i % 2 + 1) * P]
                    ins = nc.tensor.transpose(bank(j)[:, i * P:(i + 1) * P], p, ident)
                fills(ins, j)
                is_out(pe, jT(h, 0))
                is_out(pe, jT(h, 1))
                j = start(jT(h, 2))
                vs = [[VV[:, s, k, g * P:(g + 1) * P] for s in range(TT)] for k in range(2)]
                parts = [[(vs[0][0], probT(h, 0)), (vs[1][0], probT(h, 1)),
                          (vcmp[:, g, :], probT(h, 2)[0:NBLK, :])],
                         [(vs[0][0], probT(h, 4)), (vs[0][1], probT(h, 5)), (vs[1][0], probT(h, 6)),
                          (vs[1][1], probT(h, 7)), (vcmp[:, g, :], probT(h, 3)[0:NBLK, :])]]
                for t in range(TT):
                    for i, (a, b) in enumerate(parts[t]):
                        ins = mm(bank(j)[:, t * P:(t + 1) * P], a, b, i == 0, i == len(parts[t]) - 1)
                fills(ins, j)

            all_out(pe, "nq", 4)
            is_out(pe, J("ks"))
            is_out(pe, J("kw"))
            is_out(pe, J("kcmp"))
            is_out(pe, J("vcmp"))
            all_out(pe, "vs", 2)
            all_out(pe, "vw", 2)
            scores(0)
            for h in range(HEADS):
                if h + 1 < HEADS:
                    scores(h + 1)
                if h + 2 < HEADS:
                    if h % 2 == 0:
                        n = tile("mg")
                    products(start(jG(h + 2)), slot(n, (8, 512)), 256 * (h % 2), hT)
                    if h % 2 == 1:
                        done_with(n)
                weigh(h)

            all_out(pe, "OHT", 4)
            is_out(pe, jT(HEADS - 1, 2))
            for i in range(4):
                n = tile("br")
                for c in range(2):
                    chunk_pair("br", 2 * i + c, slot(n, (8, 512)), 256 * c, OHT if i < 2 else ONT)
                done_with(n)
            pe.wait_ge(S("cbc_ready"), 2)
            for i in range(2):
                modulation("g1", i, cbc2)
            pe.wait_ge(S("merged_ready"), 1)
            for i in range(2):
                n = tile("wout")
                for t in range(TT):
                    ins, j = token_half("y", 2 * i + t, slot(n, (8, 512)), 0, 512, MT, t)
                    fills(ins, j)
                done_with(n)
            for i in range(6):
                modulation("mod2", i, cbc2)
            pe.wait_ge(S("mem_normed"), 1)
            transposes("memT", memn)
            all_out(pe, "memT", 4)
            n = tile("mem")
            chunk_pair("km", 0, slot(n, (16, 256)), 0, memT)
            for t in range(TT):
                ins, j = token_half("vm", t, slot(n, (16, 256))[:, 8:16, :], 0, 256, memT, t)
                fills(ins, j)
            done_with(n)
            pe.wait_ge(S("h2_ready"), 1)
            transposes("h2T", h2)
            all_out(pe, "h2T", 4)
            n = tile("router")
            j = job("route")
            for t in range(TT):
                ins, _ = token_half("route", 0, slot(n, (8, 36)), 0, 36, hT, t, None, bank(j)[:, 36 * t:36 * t + 36], j)
            fills(ins, j)
            done_with(n)
            pe.wait_ge(S("comb_ready"), 1)
            j = job("combT")
            for t in range(TT):
                ins = nc.tensor.transpose(bank(j, rows=NE1)[:, t * P:(t + 1) * P], comb[:, t, :], ident)
            fills(ins, j)
            pe.wait_ge(S("place_ready"), 1)
            j = job("rankT1")
            for t in range(TT):
                nc.tensor.transpose(bank(j)[:, NE1 * t:NE1 * t + NE1], chosen[:, t * P:(t + 1) * P], ident[0:NE1, 0:NE1])
            fills(nc.tensor.transpose(bank(j, rows=1)[:, 64:64 + NE1], place[:, T - 1:T], ident[0:NE1, 0:NE1]), j)
            fits = is_compact(pe)
            is_out(pe, J("combT"))
            back = turn[0]
            with pe.If(fits > 0):
                for i in range(16):
                    j = job("comb", i)
                    for t in range(TT):
                        ins = mm(bank(j), h2[:, t, (i // 2) * P:(i // 2 + 1) * P],
                                 onep1[:, t, (i % 2) * 512:(i % 2) * 512 + 512], t == 0, t == TT - 1)
                    fills(ins, j)
            turn[0] = back
            with pe.If(fits < 1):
                for i in range(16):
                    j = job("comb", i)
                    for k in range(2):
                        e = 2 * i + k
                        ins = mm(bank(j)[:, k * 256:k * 256 + 256], ident[0:NE1, e:e + 1].to_broadcast([NE1, P]), combT)
                    fills(ins, j)

            for b in range(BANKS):
                j = max(q for q in range(turn[0]) if q % BANKS == b)
                is_out(pe, j)
            pe.wait_ge(S("zeros_ready"), 1)
            for b in range(4, 8):
                nc.tensor.matmul(ps[:, b * 512:b * 512 + 512], brow[0:1, 0:P], brow[0:1, 0:512], start=True,
                                 stop=True, skip_group_check=True)

            def up(turn, at, pos):
                a, b = slot(N1 + pos, (8, 512)), slot(N1 + pos + 1, (8, 512))
                late = not isinstance(turn, int)
                for m in (0, 1):
                    n = N1 + pos + m
                    pe.wait_ge(loaded[n % RING], (turn * 8 if late else 0) + load_count(n))
                for f in range(4):
                    if late or at > 0:
                        pe.wait_ge(S("hid_ready"), turn * 4 + (4 * (at - 1) + f + 1))
                    for half, wt in enumerate((a, b)):
                        for k in range(KC):
                            ins = mm(ps[:, f * 512 + half * 256:f * 512 + half * 256 + 256],
                                     wt[:, k, f * P:(f + 1) * P], hT[:, k, :], k == 0, k == KC - 1)
                    ins.then_inc(S("up_full"), 1)

            def down(turn, at, pos):
                wt = slot(N1 + pos, (4, 1024))
                n = N1 + pos
                late = not isinstance(turn, int)
                pe.wait_ge(loaded[n % RING], (turn * 8 if late else 0) + load_count(n))
                for f in range(4):
                    pe.wait_ge(S("hid_ready"), turn * 4 + (4 * at + f + 1))
                    for t in range(TT):
                        for half in range(2):
                            b = 4 + 2 * t + half
                            ins = nc.tensor.matmul(ps[:, b * 512:b * 512 + 512],
                                                   hid[:, at % 2, f, t * P:(t + 1) * P],
                                                   wt[:, f, half * 512:half * 512 + 512], start=False, stop=True,
                                                   skip_group_check=True)
                ins.then_inc(S("down_done"), 1)

            def arrived1(turn, pos):
                n = N1 + pos
                pe.wait_ge(loaded[n % RING], (0 if isinstance(turn, int) else turn * 8) + load_count(n))

            def up_compact(turn, at, pos):
                pe.wait_ge(S("xe1_ready"), turn + (at + 1))
                wt = []
                for m in range(2):
                    arrived1(turn, pos + m)
                    wt.append(slot(N1 + pos + m, (8, 512)))
                for k in range(4):
                    for q in range(4):
                        kk = 4 * (q // 2) + k
                        ins = mm(ps[32 * q:32 * q + 32, (at % 2) * 512:(at % 2) * 512 + 512], xeb[at % 2][:, kk, :],
                                 wt[q % 2][:, kk, :], k == 0, k == 3)
                ins.then_inc(S("up_full"), 4)

            def down_compact(turn, at, pos):
                u = ps[:, (at % 2) * 512:(at % 2) * 512 + 512]
                pe.wait_ge(S("gate1_ready"), turn + (at + 1))
                pe.wait_ge(S("hid1_ready"), turn + (at + 1))
                for t in range(TT):
                    nc.tensor.transpose(u[:, 256 + t * P:256 + (t + 1) * P], gateR[:, t].rearrange("p a n -> p (a n)"),
                                        ident)
                for c in range(4):
                    ins = nc.tensor.transpose(u[:, 32 * c:32 * c + 32], hid1[:, c * P:(c + 1) * P], ident[0:32, 0:32])
                ins.then_inc(S("turned1"), 1)
                pe.wait_ge(S("hidT1_ready"), turn + (at + 1))
                arrived1(turn, pos)
                wt = slot(N1 + pos, (4, 1024))
                for half in range(2):
                    for q in range(4):
                        ins = mm(ps[32 * q:32 * q + 32, 1024 + 512 * half:1536 + 512 * half],
                                 HT2[:, 32 * q:32 * q + 32], wt[:, q, half * 512:half * 512 + 512])
                ins.then_inc(S("down1_full"), 1)
                pe.wait_ge(S("ye10_ready"), turn + (at + 1))
                pe.wait_ge(S("ye11_ready"), turn + (at + 1))
                for t in range(TT):
                    for half in range(2):
                        b = 4 + 2 * t + half
                        ins = nc.tensor.matmul(ps[:, b * 512:b * 512 + 512], HT2[:, 256 + t * P:256 + (t + 1) * P],
                                               YE1[:, half * 512:half * 512 + 512], start=False, stop=True,
                                               skip_group_check=True)
                ins.then_inc(S("down_done"), 1)

            def experts1(up, down):
                up(0, 0, 0)
                up(0, 1, 2)
                down(0, 0, 4)
                with pe.Fori(0, (NE1 - 2) // 2) as i:
                    for m in range(2):
                        up(i * 2, 2 + m, 5 + 3 * m)
                        down(i * 2, 1 + m, 7 + 3 * m)
                down(0, NE1 - 1, 3 * NE1 - 1)

            with pe.If(fits > 0):
                experts1(up_compact, down_compact)
            with pe.If(fits < 1):
                experts1(up, down)
            wpos[0] = R2

            pe.wait_ge(S("mix_normed"), 1)
            transposes("h3T", xn2)
            all_out(pe, "h3T", 4)
            for i in range(5):
                n = tile("in2")
                for c in range(2):
                    chunk_pair("in2", 2 * i + c, slot(n, (8, 512)), 256 * c, hT)
                done_with(n)
            n = tile("up2")
            up2 = slot(n, (3, 384))
            pe.wait_ge(S("tanh_ready"), 2)
            for name, m, rows, src in (("w0", 0, slice(0, 64), 9), ("w1", 0, slice(64, 128), 9), ("gg", 2, slice(0, P), 11),
                                       ("a0", 1, slice(0, 64), 10), ("a1", 1, slice(64, 128), 10)):
                for i in range(2):
                    j = job(name, i)
                    for c in range(2 * i, min(3, 2 * i + 2)):
                        ins = mm(bank(j)[:, (c % 2) * 256:(c % 2) * 256 + 256], up2[rows, m, c * P:(c + 1) * P],
                                 PF[rows, src, :])
                    fills(ins, j)
            done_with(n)
            pe.wait_ge(S("masks_loaded"), 16)

            def block_sums(name, src):
                for i in range(2):
                    j = job(name, i)
                    for c in range(2 * i, min(3, 2 * i + 2)):
                        ins = mm(bank(j)[:, (c % 2) * 256:(c % 2) * 256 + 256], msk("bone"), src[:, c, :])
                    fills(ins, j)

            pe.wait_ge(S("kk_squares"), 1)
            block_sums("kks", KKs)
            for t in range(TT):
                j = job("vt", t)
                for c in range(3):
                    ins = nc.tensor.transpose(bank(j)[:, c * P:(c + 1) * P], V_[:, c, t * P:(t + 1) * P], ident)
                fills(ins, j)

            is_out(pe, J("km"))
            all_out(pe, "vm", 2)
            is_out(pe, J("in2", 0))

            def mscore(h):
                j = start(jM(f"S{h}"))
                r = slice(64 * (h % 2), 64 * (h % 2) + 64)
                for t in range(TT):
                    ins = mm(v3(bank(j), TT)[:, t, :], qa[r, h // 2, t * P:(t + 1) * P], kmT[r, h // 2, :])
                fills(ins, j)

            def mturn(h):
                pe.wait_ge(S("mem_probs"), h + 1)
                j = start(jM(f"T{h}"))
                for m in range(TT):
                    for t in range(TT):
                        ins = nc.tensor.transpose(v4(bank(j), TT, TT)[:, m, t, :], mprob(h)[:, t, m * P:(m + 1) * P], ident)
                fills(ins, j)

            def mweigh(i):
                for h in (2 * i, 2 * i + 1):
                    is_out(pe, jM(f"T{h}"))
                j = start(jM(f"O{i}"))
                for h in (2 * i, 2 * i + 1):
                    for m in range(TT):
                        ins = mm(bank(j, 256)[64 * (h % 2):64 * (h % 2) + 64, :], vm[:, m, 64 * h:64 * h + 64],
                                 mprobT(h)[:, m, :], m == 0, m == TT - 1)
                fills(ins, j)

            for f, a in ((mscore, 0), (mscore, 1), (mturn, 0), (mscore, 2), (mturn, 1), (mweigh, 0), (mscore, 3),
                         (mturn, 2), (mturn, 3), (mweigh, 1)):
                f(a)
            pe.wait_ge(S("masks_loaded"), 16)

            pe.wait_ge(S("bonus_terms"), 1)
            block_sums("bon", BON)
            for it, (d, t) in enumerate(ITS):
                pe.wait_ge(S("ends_ready"), it + 1)
                RIN = RINS[it % 2]
                for name, src in (("kk", KKIN), ("pt", PEND), ("kt", KEND)):
                    j = start(jI(it, name))
                    for c in range(3):
                        ins = nc.tensor.transpose(bank(j)[:, c * P:(c + 1) * P], src[:, c, :], ident)
                    fills(ins, j)
                for i, (a, b) in enumerate(((KKIN, PIN), (PIN, KKIN), (KIN, KKIN), (PIN, RIN), (KIN, RIN))):
                    for par in range(2):
                        j = start(jI(it, "prod", 2 * i + par))
                        r = slice(64 * par, 64 * par + 64)
                        for c in range(3):
                            ins = mm(bank(j)[:, c * P:(c + 1) * P], a[r, c, :], b[r, c, :])
                        fills(ins, j)

                def units(jj, par, a, b):
                    j = start(jj)
                    for c in range(3):
                        ins = mm(bank(j)[:, c * P:(c + 1) * P], a[:, c, :], b[:, c, :])
                    fills(ins, j)

                for lev in range(4):
                    for par in range(2):
                        pe.wait_ge(S("aot_ready"), 10 * it + 2 * (lev + 1) + par + 1)
                        if lev == 0:
                            pe.wait_ge(S("x_first"), 2 * it + par + 1)
                        else:
                            is_out(pe, jI(it, "lev", 6 * (lev - 1) + 2 + par))
                        units(jI(it, "lev", 6 * lev + par), par, unit(5, par), unit(0, par))
                    for par in range(2):
                        is_out(pe, jI(it, "lev", 6 * lev + par))
                        if lev == 0:
                            pe.wait_ge(S("xt_first"), 2 * it + par + 1)
                        else:
                            is_out(pe, jI(it, "lev", 6 * (lev - 1) + 4 + par))
                        if lev < 3:
                            units(jI(it, "lev", 6 * lev + 2 + par), par, unit(1, par), unit(2, par))
                    for par in range(2):
                        units(jI(it, "lev", 6 * lev + (4 if lev < 3 else 2) + par), par, unit(2, par), unit(1, par))
                for par in range(2):
                    is_out(pe, jI(it, "prod", 4 + par))
                j = start(jI(it, "bv"))
                for h in range(6):
                    ins = mm(bank(j)[:, 64 * h:64 * h + 64], unit(3, h % 2)[:, h // 2, :], VTOK[:, t, 64 * h:64 * h + 64])
                fills(ins, j)
                is_out(pe, jI(it, "kk"))
                is_out(pe, j)
                for par in range(2):
                    is_out(pe, jI(it, "lev", 20 + par))
                    j = start(jI(it, "wu", par))
                    for c in range(3):
                        ins = mm(bank(j)[:, c * P:(c + 1) * P], unit(1, par)[:, c, :], RHS[:, 2 * c + par, :])
                    fills(ins, j)
                is_out(pe, jI(it, "pt"))
                is_out(pe, jI(it, "kt"))
                for pc in range(3):
                    pe.wait_ge(S("pm_ready"), 3 * it + pc + 1)
                    is_out(pe, jI(it, "wu", 0))
                    is_out(pe, jI(it, "wu", 1))
                    j = start(jI(it, "gj", 2 * pc))
                    fills(mm(bank(j), AR[:, 13440 + P * pc:13568 + P * pc], PM.rearrange("p c n -> p (c n)")), j)
                    pe.wait_ge(S("um_ready"), 3 * it + pc + 1)
                    pe.wait_ge(S("vmk_ready"), 3 * it + pc + 1)
                    j = start(jI(it, "gj", 2 * pc + 1))
                    mm(bank(j), PTOK[:, pc * P:(pc + 1) * P], UM.rearrange("p c n -> p (c n)"), True, False)
                    fills(mm(bank(j), KTOK[:, pc * P:(pc + 1) * P], VMK.rearrange("p c n -> p (c n)"), False, True), j)
                for i in range(2, 5):
                    for par in range(2):
                        is_out(pe, jI(it, "prod", 2 * i + par))
                j = start(jI(it, "q"))
                for h in range(6):
                    r = slice(64 * (h % 2), 64 * (h % 2) + 64)
                    c = h // 2
                    ins = mm(bank(j)[r, c * P:(c + 1) * P], WW[:, h, :], unit(6, h % 2)[:, c, :])
                fills(ins, j)
                j = start(jI(it, "y0"))
                for h in range(6):
                    r = slice(64 * (h % 2), 64 * (h % 2) + 64)
                    c = h // 2
                    mm(bank(j)[r, c * P:(c + 1) * P], UU[:, h, :], unit(6, h % 2)[:, c, :], True, False)
                    ins = mm(bank(j)[r, c * P:(c + 1) * P], VTOK[:, t, 64 * h:64 * h + 64], unit(7, h % 2)[:, c, :], False, True)
                fills(ins, j)
                is_out(pe, jI(it, "q"))
                for i in range(6):
                    is_out(pe, jI(it, "gj", i))
                for s in range(NC4):
                    c = s if d == 0 else NC4 - 1 - s
                    n = NC4 * it + s
                    if s == 0:
                        if it % 2 == 0:
                            pe.wait_ge(S("state_zero"), it // 2 + 1)
                    else:
                        is_out(pe, jI(it, "rec", 2 * s - 1))
                    j = start(jI(it, "rec", 2 * s))
                    for pc in range(3):
                        ins = mm(bank(j)[:, 32 * pc:32 * pc + 32], HS[n % 2][:, pc, :], RIN[:, pc, 32 * c:32 * c + 32])
                    fills(ins, j)
                    j = start(jI(it, "rec", 2 * s + 1))
                    for pc in range(3):
                        ins = mm(bank(j)[:, P * pc:P * pc + P], GB[:, pc, c, :], HS[n % 2][:, pc, :])
                    fills(ins, j)
                is_out(pe, jI(it, "rec", 7))
            ones_square = C("scan")[:, 1:2].to_broadcast([P, P])

            def channel_sums(name, src, ready):
                pe.wait_ge(S(ready), 1)
                j = job(name)
                for c in range(3):
                    ins = mm(bank(j, 256), ones_square, src[:, c, :], c == 0, c == 2)
                fills(ins, j)

            channel_sums("cmean", CV, "conv_done")
            pe.wait_ge(S("y_done"), 1)
            block_sums("gn1", YY)
            outs = [(tile("wout2"), [job("y2", 2 * i + t) for t in range(TT)]) for i in range(2)]

            def project(k0, k1):
                for n, js in outs:
                    for t, j in enumerate(js):
                        for k in range(k0, k1):
                            ins = mm(bank(j), MIX[:, k, t * P:(t + 1) * P], slot(n, (8, 512))[:, k, :], k == 0, k == 7)
                        if k1 == KC:
                            fills(ins, j)

            for i in range(2):
                is_out(pe, jM(f"O{i}"))
            project(0, 2)
            channel_sums("cvar", CS, "conv_centred")
            pe.wait_ge(S("gn_squares"), 1)
            block_sums("gn2", c3(3072))
            pe.wait_ge(S("conv_ready"), 1)
            project(2, 5)
            pe.wait_ge(S("mix_ready"), 1)
            project(5, KC)
            for n, js in outs:
                is_full(pe, js[-1])
                pe.sem_inc(freed[n % RING], 1)
            pe.wait_ge(S("xf_ready"), 1)
            transposes("h4T", xf)
            all_out(pe, "h4T", 4)
            n = tile("router2")
            j = job("aff")
            for t in range(TT):
                ins, _ = token_half("aff", 0, slot(n, (8, 16)), 0, 16, hT, t, None, bank(j)[:, 16 * t:16 * t + 16], j)
            fills(ins, j)
            done_with(n)
            pe.wait_ge(S("aff_ready"), 1)
            j = job("affT")
            for t in range(TT):
                ins = nc.tensor.transpose(bank(j, rows=NE2)[:, t * P:(t + 1) * P], aff[:, t, :], ident)
            fills(ins, j)
            pe.wait_ge(S("rank_ready"), 1)
            j = job("rankT")
            for t in range(TT):
                ins = nc.tensor.transpose(bank(j)[:, 16 * t:16 * t + 16], sel[:, t * P:(t + 1) * P], ident[0:NE2, 0:NE2])
            fills(ins, j)
            pe.wait_ge(S("onehot_ready"), 1)
            for k in range(KC):
                j = job("xe", k)
                for t in range(TT):
                    ins = mm(bank(j), xf[:, t, k * P:(k + 1) * P], onep[:, t, :], t == 0, t == TT - 1)
                fills(ins, j)
            for b in range(BANKS):
                is_out(pe, max(q for q in range(turn[0]) if q % BANKS == b))
            pe.wait_ge(S("zeros2_ready"), 1)
            for b in range(4, 8):
                nc.tensor.matmul(ps[:, b * 512:b * 512 + 512], zrow[:, 0:P], zrow, start=True, stop=True,
                                 skip_group_check=True)
            pe.sem_inc(S("up2_tiles"), UP0)
            pe.sem_inc(S("turned2"), 1)
            with pe.Fori(0, NE2 // 4) as i:
                for m in range(4):
                    pe.wait_ge(S("xe_ready"), i * 4 + (m + 1))
                    u = ps[:, (m % 2) * 512:(m % 2) * 512 + 512]
                    for half in range(2):
                        wt = []
                        for g in range(2):
                            n = N2 + 6 * m + 2 * half + g
                            pe.wait_ge(loaded[n % RING], i * 64 + load_count(n))
                            wt.append(slot(n, (4, 1024)))
                        for k in range(4):
                            for q in range(4):
                                ins = mm(u[32 * q:32 * q + 32, :], xeb[m % 2][:, 4 * half + k, :],
                                         wt[q // 2][:, k, (q % 2) * 512:(q % 2) * 512 + 512],
                                         half == 0 and k == 0, half == 1 and k == 3)
                        ins.then_inc(S("up2_tiles"), 1)
                    pe.wait_ge(S("hid2_ready"), i * 4 + (m + 1))
                    pe.wait_ge(S("gate_ready"), i * 4 + (m + 1))
                    for t in range(TT):
                        nc.tensor.transpose(u[:, 256 + t * P:256 + (t + 1) * P], gateR[:, t].rearrange("p a n -> p (a n)"),
                                            ident)
                    for c in range(4):
                        ins = nc.tensor.transpose(u[:, 64 * c:64 * c + 64], hid2[:, c * P:(c + 1) * P], ident[0:64, 0:64])
                    ins.then_inc(S("turned2"), 1)
                    pe.wait_ge(S("hidT_ready"), i * 4 + (m + 1))
                    for part in range(2):
                        n = N2 + 6 * m + 4 + part
                        pe.wait_ge(loaded[n % RING], i * 64 + load_count(n))
                        for half in range(2):
                            for q in range(4):
                                ins = mm(ps[32 * q:32 * q + 32, 1024 + 512 * half:1536 + 512 * half],
                                         HT2[:, 64 * q + 32 * part:64 * q + 32 * part + 32],
                                         slot(n, (4, 1024))[:, q, half * 512:half * 512 + 512], part == 0, part == 1)
                        ins.then_inc(S("down2_tiles"), 1)
                    pe.wait_ge(S("ye0_ready"), i * 4 + (m + 1))
                    pe.wait_ge(S("ye1_ready"), i * 4 + (m + 1))
                    for t in range(TT):
                        for half in range(2):
                            b = 4 + 2 * t + half
                            ins = nc.tensor.matmul(ps[:, b * 512:b * 512 + 512], HT2[:, 256 + t * P:256 + (t + 1) * P],
                                                   YE[:, half * 512:half * 512 + 512], start=False, stop=True,
                                                   skip_group_check=True)
            nc.tensor.matmul(ps[0:1, 0:1], ident[0:1, 0:1], ident[0:1, 0:1], start=True, stop=True)\
                .then_inc(S("comb2_done"), 1)

        @block.vector
        def _(dve):
            steps = [0]

            def link(ins):
                steps[0] += 1
                ins.then_inc(S("dve_step"), 1)
                dve.wait_ge(S("dve_step"), steps[0])

            said = {}

            def say(ins, name):
                said[name] = said.get(name, 0) + 1
                ins.then_inc(S(name), 1)
                dve.wait_ge(S(name), said[name])

            def carried(ins, j):
                frees(ins, j)
                is_out(dve, j)

            tt, ts, stt = nc.vector.tensor_tensor, nc.vector.tensor_scalar, nc.vector.scalar_tensor_tensor
            cp = nc.vector.tensor_copy

            def rsqrt(ins):
                say(ins, "variance_ready")
                dve.wait_ge(S("rstd_ready"), said["variance_ready"])

            def norm_stats(src, eps=1e-5):
                norm_stats_only(src)
                rsqrt(ts(rstd, mv[:, :, 1], eps, None, ALU.add))

            def norm_stats_only(src):
                for t in range(TT):
                    for c in range(2):
                        ins = nc.vector.bn_stats(bns[:, t, c, :], src[:, t, c * 512:(c + 1) * 512])
                link(ins)
                for t in range(TT):
                    ins = nc.vector.bn_aggr(mv[:, t, :], bns[:, t].rearrange("p c s -> p (c s)"))
                link(ins)

            def layer_norm(dst, src):
                norm_stats(src)
                for t in range(TT):
                    ins = ts(dst[:, t, :], src[:, t, :], mv[:, t, 0:1], rstd[:, t:t + 1], ALU.subtract, ALU.mult)
                link(ins)

            def affine(dst, scale, shift, name):
                link(tt(dst[:], dst[:], mid(scale, TT), ALU.mult))
                say(tt(dst[:], dst[:], mid(shift, TT), ALU.add), name)

            dve.wait_ge(S("c_silu"), 1)
            say(cp(cbc, last(ccol[:, 0:8], P)), "cbc_ready")
            dve.wait_ge(S("x_loaded"), 16)
            layer_norm(xn, x)
            for i in range(4):
                j = J("mod", i)
                is_full(dve, j)
                carried(cp(mod1[:, i // 2, (i % 2) * 512:(i % 2) * 512 + 512], bank(j)), j)
            for t in range(TT):
                link(stt(xn[:, t, :], mod1[:, 1, :], 1.0, xn[:, t, :], ALU.add, ALU.mult))
            say(tt(xn[:], xn[:], mid(mod1[:, 0, :], TT), ALU.add), "h_ready")

            is_out(dve, J("cols"))
            say(tt(lb, colv[:, VA["l0"]:VA["l0"] + 8], colv[:, VA["l1"]:VA["l1"] + 8], ALU.subtract), "lb_logit")
            dve.wait_ge(S("lb_sigmoid"), 1)
            link(ts(omlb, lb, -1.0, 1.0, ALU.mult, ALU.add))
            all_out(dve, "f", 4)
            for h in range(HEADS):
                ins = ts(F[:, h, :], F[:, h, :], omlb[:, h:h + 1], lb[:, h:h + 1], ALU.mult, ALU.add)
            say(ins, "f_ready")
            for i in range(4):
                j = J("v", i)
                is_full(dve, j)
                frees(cp(V[:, i % 2, (i // 2) * 512:(i // 2) * 512 + 512], bank(j)), j)
            dve.wait_ge(S("log_ready"), 1)
            ins = ts(F[:], F[:], -1.0, 1.0, ALU.mult, ALU.add)
            for h in range(HEADS):
                ins = nc.vector.tensor_tensor_scan(B[:, h, :], C("scan"), L[:, h, :], 0.0, ALU.mult, ALU.add)
            say(ins, "cumsum_ready")
            all_out(dve, "kvc", 2)
            for i in range(2):
                nc.vector.memset(blocks[i][:, 960:962], 0.0)
                for g in range(2):
                    src = kvc[:, 2 * i + g, :]
                    src = bass.AP(src.tensor, src.offset, [src.ap[0], [1, 32], [16, NBLK]])
                    ins = tt(v4(blocks[i][:, 0:960], 32, 2)[:, :, g, :], src, last(colv[:, 384 + 32 * i:416 + 32 * i], NBLK), ALU.add)
                say(ins, "blocks_ready")
            dve.wait_ge(S("exp_ready"), 2)
            all_out(dve, "q", 4)
            tt(Q[:], Q[:], L[:], ALU.mult)
            cp(dec, L[:, :, CHUNK - 1::CHUNK])
            link(tt(KI[:], F[:], E[:], ALU.mult))
            say(tt(KE.rearrange("p h (c j) -> p (h c) j", j=CHUNK), KI.rearrange("p h (c j) -> p (h c) j", j=CHUNK),
                   last(st[:, 48:112], CHUNK), ALU.mult), "ke_ready")
            for i in range(4):
                j = J("att", i)
                is_full(dve, j)
                frees(tt(AT[:, 4 * i:4 * i + 4, :], v3(bank(j), 4), mid(C("upto"), 4), ALU.mult), j)
            is_full(dve, J("vcmp"))
            for h in range(HEADS):
                if h >= 2:
                    is_full(dve, jO(h - 2))
                s = SH[:, h % 2]
                for t in range(TT):
                    j = jU(h, t)
                    is_full(dve, j)
                    for c in range(NC4):
                        n = NC4 * t + c
                        u = v3(bank(j), NC4)[:, c, :]
                        if n == 0:
                            link(cp(s[:, 1, :], u))
                        elif n < 7:
                            ins = stt(s[:, n + 1, :], s[:, n, :], dec[:, h, n:n + 1], u, ALU.mult, ALU.add)
                            if c == NC4 - 1:
                                carried(ins, j)
                            elif n == 6:
                                say(ins, "states_ready")
                            else:
                                link(ins)
                    if t == 1:
                        dve.sem_inc(free[j % BANKS], 1)
            all_out_heads(dve)
            Of = arena(1)
            all_out(dve, "g", 4)
            rsqrt(ts(st[:, 150:166], st[:, 150:166], 1.0 / P, 1e-6, ALU.mult, ALU.add))
            link(tt(arena(1).rearrange("p (u v) -> p u v", v=P), arena(1).rearrange("p (u v) -> p u v", v=P),
                    last(st[:, 150:166], P), ALU.mult))
            say(tt(Of, Of, arena(6), ALU.mult), "heads_normed")

            is_out(dve, J("gate"))
            link(tt(gates[:, :, 0::3], gates[:, :, 0::3], last(C("seen"), HEADS), ALU.mult))
            dve.wait_ge(S("bias_loaded"), 48)

            def mask_bias(h0, h1):
                b = BM[:, h0:h1].rearrange("p h t k -> p h (t k)")
                link(tt(b, b, mid(neg, h1 - h0), ALU.add))

            SC = P ** -0.5

            def softmax_in(h):
                if h >= 2:
                    is_full(dve, jT(h - 2, 1))
                j = jS(h, 0)
                is_full(dve, j)
                for t in range(TT):
                    ins = stt(prob(h, t, 0), bank(j)[:, NBLK * t:NBLK * t + NBLK], SC, BM[:, h, t, 31::16],
                              ALU.mult, ALU.add)
                carried(ins, j)
                for t in range(TT):
                    j = jS(h, 1 + t)
                    n = P * (t + 1)
                    is_full(dve, j)
                    p = probs(h)[:, 256 * t:256 * t + 2 * n]
                    carried(stt(v3(p, 2), v3(bank(j, 2 * n), 2), SC, mid(BM[:, h, t, 0:n], 2), ALU.mult, ALU.add), j)
                    nc.vector.tensor_reduce(nmx[:, h % 2, t, 1:3], v3(p, 2), AX.X, ALU.max, negate=True)
                say(nc.vector.tensor_reduce(nmx[:, h % 2, :, 0], v3(probs(h)[:, 768:798], 2), AX.X, ALU.max,
                                            negate=True), "scores_ready")

            def softmax_out(h):
                dve.wait_ge(S("exps_ready"), h + 1)
                link(nc.vector.reciprocal(rs[:, h % 2], sums[:, h % 2]))
                link(tt(rs[:, h % 2], rs[:, h % 2], gates[:, :, 3 * h:3 * h + 3], ALU.mult))
                for t in range(TT):
                    for kind in range(3):
                        p = prob(h, t, kind)
                        ins = ts(p, p, rs[:, h % 2, t, kind:kind + 1], None, ALU.mult)
                say(ins, "probs_ready")

            mask_bias(0, 1)
            softmax_in(0)
            mask_bias(1, HEADS)
            for h in range(HEADS):
                if h + 1 < HEADS:
                    softmax_in(h + 1)
                softmax_out(h)

            is_full(dve, jT(HEADS - 1, 2))
            say(cp(cbc2, last(ccol[:, 0:8], P)), "cbc_ready")
            for h in range(HEADS):
                is_out(dve, jG(h))
            for i in range(4):
                j = J("br", i)
                is_full(dve, j)
                carried(tt(MT[:, 2 * i:2 * i + 2, :], mgh[:, 2 * i:2 * i + 2, :], v3(bank(j), 2), ALU.mult), j)
            for i in range(4):
                j = J("br", 4 + i)
                is_full(dve, j)
                carried(tt(mgn[:, 2 * i:2 * i + 2, :], mgn[:, 2 * i:2 * i + 2, :], v3(bank(j), 2), ALU.mult), j)
            say(tt(MT[:], MT[:], mgn[:], ALU.add), "merged_ready")
            def rms_norm(dst, src, name):
                norm_stats_only(src)
                link(tt(rstd, mv[:, :, 0], mv[:, :, 0], ALU.mult))
                link(tt(rstd, rstd, mv[:, :, 1], ALU.add))
                rsqrt(ts(rstd, rstd, 1e-6, None, ALU.add))
                for t in range(TT):
                    ins = ts(dst[:, t, :], src[:, t, :], rstd[:, t:t + 1], None, ALU.mult)
                if name:
                    say(ins, name)
                else:
                    link(ins)

            dve.wait_ge(S("mem_loaded"), 16)
            rms_norm(memn, memn, "mem_normed")
            all_out(dve, "g1", 2)

            def residual(j, gate, t, half, src):
                c = slice(half * 512, half * 512 + 512)
                ins = stt(tmp, mod2[:, gate, c], 1.0, src, ALU.add, ALU.mult)
                if j is None:
                    link(ins)
                else:
                    carried(ins, j)
                link(stt(x[:, t, c], x[:, t, c], ALPHA, tmp, ALU.mult, ALU.add))

            for i in range(4):
                is_full(dve, J("y", i))
                residual(J("y", i), 0, i % 2, i // 2, bank(J("y", i)))
            layer_norm(x, x)
            dve.wait_ge(S("ln1_loaded"), 32)
            affine(x, lnr[:, 0, :], lnr[:, 1, :], "x1_ready")
            layer_norm(h2, x)
            all_out(dve, "mod2", 6)
            for t in range(TT):
                link(stt(h2[:, t, :], mod2[:, 2, :], 1.0, h2[:, t, :], ALU.add, ALU.mult))
            say(tt(h2[:], h2[:], mid(mod2[:, 1, :], TT), ALU.add), "h2_ready")

            j = J("route")
            is_full(dve, j)
            dve.wait_ge(S("router_bias_loaded"), 32)
            carried(tt(lg, v3(bank(j, 72), TT), mid(rbias[:], TT), ALU.add), j)
            gl, el = lg[:, :, 0:4], lg[:, :, 4:36]
            link(nc.vector.tensor_reduce(gmax, gl, AX.X, ALU.max))
            link(tt(oh4, gl, last(gmax, 4), ALU.is_equal))
            link(tt(oh4, oh4, mid(C("gkey"), TT), ALU.mult))
            link(nc.vector.tensor_reduce(gkm, oh4, AX.X, ALU.max))
            link(tt(oh4, mid(C("gkey"), TT), last(gkm, 4), ALU.is_equal))
            say(tt(rt_exp, gl, last(gmax, 4), ALU.subtract), "route_max")
            link(ts(oh4, oh4, -2 * NEG, NEG, ALU.mult, ALU.add))
            for t in range(TT):
                ins = tt(v3(el2[:, t, :], 4), v3(el[:, t, :], 4), last(oh4[:, t, :], 8), ALU.min)
            link(ins)
            for n, (m, oh) in enumerate(((m1, oh1), (m2, oh2))):
                link(nc.vector.tensor_reduce(m, el2, AX.X, ALU.max))
                link(tt(oh, el2, last(m, NE1), ALU.is_equal))
                link(tt(oh, oh, mid(C("ekey"), TT), ALU.mult))
                link(nc.vector.tensor_reduce(gkm, oh, AX.X, ALU.max))
                link(tt(oh, mid(C("ekey"), TT), last(gkm, NE1), ALU.is_equal))
                if n == 0:
                    link(stt(el2, oh, 2 * NEG, el2, ALU.mult, ALU.add))
            say(tt(rt_d, m2, m1, ALU.subtract), "route_top")
            dve.wait_ge(S("route_exp"), 2)
            link(nc.vector.tensor_reduce(gmax, rt_exp, AX.X, ALU.add))
            link(ts(m1, rt_d, 1.0, None, ALU.add))
            link(tt(gmax, gmax, m1, ALU.mult))
            link(nc.vector.reciprocal(gmax, gmax))
            link(tt(rt_d, rt_d, gmax, ALU.mult))
            link(tt(oh1, oh1, last(gmax, NE1), ALU.mult))
            link(tt(oh2, oh2, last(rt_d, NE1), ALU.mult))
            say(tt(comb, oh1, oh2, ALU.add), "comb_ready")
            say(nc.vector.memset(brow[0:1, 0:512], 0.0), "zeros_ready")
            is_out(dve, J("combT"))
            nc.vector.memset(ones1, 1.0)
            link(ts(chosen, combT, 0.0, None, ALU.is_gt))
            link(nc.vector.tensor_tensor_scan(place, ones1, chosen, 0.0, ALU.mult, ALU.add))
            link(tt(chosen, chosen, place, ALU.mult))
            say(ts(chosen, chosen, -1.0, None, ALU.add), "place_ready")
            j = J("rankT1")
            is_full(dve, j)
            link(nc.vector.tensor_reduce(most, bank(j, rows=1)[:, 64:64 + NE1], AX.X, ALU.max))
            ts(compact[0:1, 0:1], most, float(CAP1), None, ALU.is_le)
            carried(ts(rank1, v3(bank(j, 64), TT), -1.0, float(NE1), ALU.mult, ALU.add), j)
            for t in range(TT):
                ins = tt(v3(onep1[:, t, :], NE1), last(rank1[:, t, :], CAP1), mid(C("ekey"), NE1), ALU.is_equal)
            link(ins)
            for t in range(TT):
                ins = tt(v3(gatep1[:, t, :], NE1), v3(onep1[:, t, :], NE1), last(comb[:, t, :], CAP1), ALU.mult)
            say(ins, "spread_ready")
            fits = dve.value_load(compact[0:1, 0:1], min_val=0, max_val=1)
            all_out(dve, "comb", 16)

            def hidden(turn, at):
                late = not isinstance(turn, int)
                wb = WB[:, turn + at, :]
                for f in range(4):
                    dve.wait_ge(S("silu_ready"), turn * 4 + (4 * at + f + 1))
                    if f == 0 and (late or at > 1):
                        dve.wait_ge(S("down_done"), turn + (at - 1))
                    tt(hid[:, at % 2, f, :], silu[:, f, :], wb, ALU.mult).then_inc(S("hid_step"), 1)
                    dve.wait_ge(S("hid_step"), turn * 4 + (4 * at + f + 1))
                    tt(hid[:, at % 2, f, :], hid[:, at % 2, f, :], ps[:, f * 512 + 256:f * 512 + 512], ALU.mult)\
                        .then_inc(S("hid_ready"), 1)

            with dve.If(fits > 0):
                with dve.Fori(0, NE1 // 2) as i:
                    for m in range(2):
                        u = ps[:, m * 512:m * 512 + 512]
                        dve.wait_ge(S("up_full"), i * 8 + 4 * (m + 1))
                        cp(part1, u[64:128]).then_inc(S("part_ready"), 1)
                        dve.wait_ge(S("part_ready"), i * 2 + (m + 1))
                        tt(sum1, u[0:64], part1, ALU.add).then_inc(S("sum1_ready"), 1)
                        dve.wait_ge(S("silu1_ready"), i * 2 + (m + 1))
                        tt(hid1, sg1, sum1[32:64], ALU.mult).then_inc(S("hid1_ready"), 1)
                        dve.wait_ge(S("down1_full"), i * 2 + (m + 1))
                        cp(YE1[:, 512:1024], ps[:, 1536:2048]).then_inc(S("ye11_ready"), 1)
            with dve.If(fits < 1):
                hidden(0, 0)
                hidden(0, 1)
                with dve.Fori(0, (NE1 - 2) // 2) as i:
                    hidden(i * 2, 2)
                    hidden(i * 2, 3)
            dve.wait_ge(S("down_done"), NE1)
            for t in range(TT):
                for half in range(2):
                    b = 4 + 2 * t + half
                    residual(None, 3, t, half, ps[:, b * 512:b * 512 + 512])
            layer_norm(x, x)
            dve.wait_ge(S("ln2_loaded"), 32)
            affine(x, lnr2[:, 0, :], lnr2[:, 1, :], "x2_ready")

            rms_norm(xn2, x, "mix_normed")
            is_full(dve, J("h3T", 3))
            nc.vector.memset(PR[:, :, 0:1], 0.0)
            nc.vector.memset(PR[:, :, 257:258], 0.0).then_inc(S("pads_ready"), 1)
            link(tt(shift0, colv[:, 128:140], colv[:, 140:152], ALU.add))
            link(ts(shift0, shift0, -1.0, 1.0, ALU.mult, ALU.add))

            def mem_scores(h):
                j = jM(f"S{h}")
                is_full(dve, j)
                if h >= 2:
                    is_full(dve, jM(f"T{h - 2}"))
                carried(ts(mprob(h), v3(bank(j), TT), 0.125, None, ALU.mult), j)
                say(nc.vector.tensor_reduce(mmax[:, h % 2, :], mprob(h), AX.X, ALU.max, negate=True), "mem_scores")

            def mem_probs(h):
                dve.wait_ge(S("mem_exps"), h + 1)
                link(nc.vector.reciprocal(msum[:, h % 2, :], msum[:, h % 2, :]))
                say(tt(mprob(h), mprob(h), last(msum[:, h % 2, :], T), ALU.mult), "mem_probs")

            for i in range(6):
                is_out(dve, J("in2", 4 + i))
                cs = (2 * i, 2 * i + 1)
                for c in cs:
                    ins = ts(PF[:, c, :], PR[:, c, 1:257], shift0[:, c:c + 1], None, ALU.mult)
                link(ins)
                for c in cs:
                    ins = stt(PF[:, c, :], PR[:, c, 0:256], col(1, VB["mu0"] + c), PF[:, c, :], ALU.mult, ALU.add)
                link(ins)
                for c in cs:
                    ins = stt(PF[:, c, :], PR[:, c, 2:258], col(1, VB["mu1"] + c), PF[:, c, :], ALU.mult, ALU.add)
                if i < 5:
                    link(ins)
            say(ins, "shifted")
            for c in range(3):
                ins = ts(KKn[:, c, :], K_[:, c, :], col(1, VB["kk"] + c), None, ALU.mult)
            link(ins)
            say(tt(KKs, KKn, KKn, ALU.mult), "kk_squares")

            taps = [0]

            def convolve(n):
                for k in range(taps[0], min(31, taps[0] + n)):
                    if k:
                        dve.wait_ge(S("tap_done"), k)
                    for c in range(3):
                        a, u = col(2, 3 * k + c), CU[:, c, k:k + 256]
                        if k == 0:
                            ins = ts(CV[:, c, :], u, a, col(1, VB["cb"] + c), ALU.mult, ALU.add)
                        else:
                            ins = stt(CV[:, c, :], u, a, CV[:, c, :], ALU.mult, ALU.add)
                    ins.then_inc(S("conv_done" if k == 30 else "tap_done"), 1)
                    taps[0] = k + 1

            for i in range(2):
                n = 2 - i
                j = J("kks", i)
                is_full(dve, j)
                frees(ts(KKs[:, 2 * i:2 * i + n, :], v3(bank(j, 256 * n), n), 1e-12, None, ALU.add), j)
                is_out(dve, j)
                dve.sem_inc(S("kk_sums"), 1)
            def prepare(it, part):
                d, t = ITS[it]
                RIN = RINS[it % 2]
                tk = slice(t * P, (t + 1) * P)
                sg = SG[d][:, :, tk]
                if part == 0:
                    bi = BI if d == 0 else TM
                    for c in range(3):
                        ins = nc.vector.tensor_tensor_scan(bi[:, c, :], C("scan")[:, 0:P], sg[:, c, :], 0.0, ALU.mult,
                                                           ALU.add)
                    link(ins)
                    link(cp(decc, bi[:, :, CHUNK - 1::CHUNK]))
                    if d == 0:
                        say(tt(BP, bi, sg, ALU.subtract), "decays_ready")
                    else:
                        for c in range(3):
                            ins = tt(v3(BP[:, c, :], NC4), last(decc[:, c, :], CHUNK), v3(bi[:, c, :], NC4), ALU.subtract)
                        link(ins)
                        say(tt(BI, BP, sg, ALU.add), "decays_ready")
                elif part == 1:
                    dve.wait_ge(S("decay_exps"), it + 1)
                    tt(RIN, RIN, R_[:, :, tk], ALU.mult)
                    tt(KKIN, KKIN, KKn[:, :, tk], ALU.mult)
                    for c in range(3):
                        ts(BP[:, c, :], AA[d][:, c, tk], col(1, ka + c), st[:, 108 + c:109 + c], ALU.mult, ALU.add)
                    link(tt(TM, KKn[:, :, tk], AA[d][:, :, tk], ALU.mult))
                elif part == 2:
                    tt(PIN, TM, KIN, ALU.mult)
                    link(tt(BP, BP, K_[:, :, tk], ALU.mult))
                    link(tt(KIN, KIN, BP, ALU.mult))
                else:
                    for c in range(3):
                        for a, b in ((PEND, PIN), (KEND, KIN)):
                            ins = tt(v3(a[:, c, :], NC4), v3(b[:, c, :], NC4), last(decc[:, c, :], CHUNK), ALU.mult)
                    say(ins, "ends_ready")

            ka = VB["ka"]
            link(ts(st[:, 108:111], colv[:, 128 + ka:131 + ka], -1.0, 1.0, ALU.mult, ALU.add))
            link(ts(st[:, 111:114], st[:, 108:111], 2.0, None, ALU.mult))
            mem_scores(0)
            mem_scores(1)
            nc.vector.memset(CU[:, :, 0:15], 0.0)
            nc.vector.memset(CU[:, :, 271:286], 0.0)
            link(tt(CU[:, :, 15:271], CA, CS, ALU.mult))
            all_out(dve, "a0", 2)
            all_out(dve, "a1", 2)
            link(tt(BON, AA[0], AA[1], ALU.add))
            mem_probs(0)
            mem_scores(2)
            for c in range(3):
                ins = ts(BON[:, c, :], BON[:, c, :], col(1, ka + c), st[:, 111 + c:112 + c], ALU.mult, ALU.add)
            link(ins)
            link(tt(BON, BON, K_, ALU.mult))
            mem_probs(1)
            mem_scores(3)
            prepare(0, 0)
            mem_probs(2)
            dve.wait_ge(S("kk_roots"), 2)
            link(nc.vector.reciprocal(KKs, KKs))
            for c in range(3):
                ins = stt(BON[:, c, :], R_[:, c, :], col(1, VB["rk"] + c), BON[:, c, :], ALU.mult, ALU.mult)
            say(ins, "bonus_terms")
            mem_probs(3)
            link(tt(KKn, KKn, KKs, ALU.mult))

            for part in range(1, 4):
                prepare(0, part)
            for i in range(2):
                n = 2 - i
                j = J("bon", i)
                is_full(dve, j)
                if i == 0:
                    is_full(dve, J("bon", 1))
                frees(tt(BON[:, 2 * i:2 * i + n, :], V_[:, 2 * i:2 * i + n, :], v3(bank(j, 256 * n), n), ALU.mult), j)
            for it, (d, t) in enumerate(ITS):
                tk = slice(t * P, (t + 1) * P)
                RIN = RINS[it % 2]
                if it % 2 == 0:
                    dve.wait_ge(S("masks_loaded"), 16 * (it // 2 + 1))
                    say(nc.vector.memset(HS[0], 0.0), "state_zero")
                for par in range(2):
                    j = jI(it, "prod", par)
                    is_full(dve, j)
                    carried(tt(unit(0, par), v3(bank(j, 384), 3), mid(msk(f"merge1_{d}", d), 3), ALU.mult), j)
                    say(tt(unit(0, par), unit(0, par), mid(ident, 3), ALU.add), "x_first")
                for i, (u, m) in enumerate(((4, "strictT"), (3, "strictT"), (6, "uptoT"), (7, "uptoT"))):
                    for par in range(2):
                        j = jI(it, "prod", 2 + 2 * i + par)
                        is_full(dve, j)
                        ins = tt(unit(u, par), v3(bank(j, 384), 3), mid(msk(f"{m}{d}", d), 3), ALU.mult)
                        frees(ins, j)
                        if u == 4:
                            is_out(dve, j)
                            dve.sem_inc(S("at_ready"), 1)
                for lev in range(4):
                    convolve(1)
                    for q in ((0, 1) if lev < 3 else (1,)):
                        for par in range(2):
                            j = jI(it, "lev", 6 * lev + 2 + (2 * q if lev < 3 else 0) + par)
                            is_full(dve, j)
                            if lev == 0 and q == 1:
                                dve.wait_ge(S("xt_first"), 2 * it + par + 1)
                            carried(tt(unit(q, par), unit(q, par), v3(bank(j, 384), 3), ALU.add), j)
                convolve(3)
                if it == 0:
                    all_out(dve, "vt", 2)
                for pc in range(3):
                    if pc:
                        is_full(dve, jI(it, "gj", 2 * pc - 1))
                    tt(VMK, mid(VTOK[:, t, pc * P:(pc + 1) * P], NC4), last(C("chunk"), P), ALU.mult)\
                        .then_inc(S("vmk_ready"), 1)
                    link(tt(DG, mid(ident, NC4), last(decc[:, pc, :], P), ALU.mult))
                    j = jI(it, "gj", 2 * pc)
                    is_full(dve, j)
                    link(tt(GB[:, pc], v3(bank(j), NC4), mid(msk("bone"), NC4), ALU.mult))
                    carried(tt(GB[:, pc], GB[:, pc], DG, ALU.add), j)
                    j = jI(it, "gj", 2 * pc + 1)
                    is_full(dve, j)
                    carried(tt(JB[:, pc], v3(bank(j), NC4), mid(msk("bone"), NC4), ALU.mult), j)
                convolve(1)
                j = jI(it, "q")
                is_full(dve, j)
                carried(tt(RIN, RIN, v3(bank(j, 384), 3), ALU.add), j)
                j = jI(it, "y0")
                is_full(dve, j)
                y = YY[:, :, tk]
                if d == 0:
                    carried(cp(y, v3(bank(j, 384), 3)), j)
                else:
                    carried(tt(y, y, v3(bank(j, 384), 3), ALU.add), j)
                for s in range(NC4):
                    c = s if d == 0 else NC4 - 1 - s
                    n = NC4 * it + s
                    j = jI(it, "rec", 2 * s + 1)
                    is_full(dve, j)
                    carried(tt(HS[(n + 1) % 2], v3(bank(j, 384), 3), JB[:, :, c, :], ALU.add), j)
                    j = jI(it, "rec", 2 * s)
                    yc = y[:, :, 32 * c:32 * c + 32]
                    carried(tt(yc, yc, v3(bank(j, 96), 3), ALU.add), j)
                    if it + 1 < len(ITS):
                        prepare(it + 1, s)
                if it == 1:
                    dve.sem_inc(S("masks_used"), 1)
            dve.sem_inc(S("y_done"), 1)
            j = J("cmean")
            is_full(dve, j)
            link(ts(TMc, bank(j, 256), 1.0 / 384, None, ALU.mult))
            dve.sem_inc(free[j % BANKS], 1)
            link(tt(CV, CV, mid(TMc, 3), ALU.subtract))
            say(tt(CS, CV, CV, ALU.mult), "conv_centred")
            for i in range(2):
                n = 2 - i
                j = J("gn1", i)
                is_full(dve, j)
                if i == 0:
                    is_full(dve, J("gn1", 1))
                carried(stt(YY[:, 2 * i:2 * i + n, :], v3(bank(j, 256 * n), n), -1.0 / 64, YY[:, 2 * i:2 * i + n, :],
                            ALU.mult, ALU.add), j)
            GS = c3(3072)
            say(tt(GS, YY, YY, ALU.mult), "gn_squares")
            j = J("cvar")
            is_full(dve, j)
            frees(ts(CS[:, 0, :], bank(j, 256), 1.0 / 384, 1e-5, ALU.mult, ALU.add), j)
            is_out(dve, j)
            dve.sem_inc(S("conv_var"), 1)
            is_full(dve, J("gn2", 1))
            for i in range(2):
                n = 2 - i
                j = J("gn2", i)
                carried(ts(GS[:, 2 * i:2 * i + n, :], v3(bank(j, 256 * n), n), 1.0 / 64, 64e-5, ALU.mult, ALU.add), j)
            dve.sem_inc(S("gn_var"), 1)
            dve.wait_ge(S("conv_root"), 1)
            link(nc.vector.reciprocal(CS[:, 0, :], CS[:, 0, :]))
            say(tt(CV, CV, mid(CS[:, 0, :], 3), ALU.mult), "conv_normed")
            dve.wait_ge(S("gn_root"), 1)
            link(nc.vector.reciprocal(GS, GS))
            link(tt(YY, YY, GS, ALU.mult))
            for c in range(3):
                ins = ts(YY[:, c, :], YY[:, c, :], col(1, VB["lxg"] + c), col(1, VB["lxb"] + c), ALU.mult, ALU.add)
            link(ins)
            link(tt(YY, YY, BON, ALU.add))
            say(tt(MIX[:, 5:8, :], YY, GG, ALU.mult), "mix_ready")
            for i in range(4):
                j = J("y2", i)
                is_full(dve, j)
                c = slice((i // 2) * 512, (i // 2) * 512 + 512)
                carried(tt(x[:, i % 2, c], x[:, i % 2, c], bank(j), ALU.add), j)
            rms_norm(xf, x, "xf_ready")
            j = J("aff")
            is_full(dve, j)
            carried(cp(aff, v3(bank(j, 32), TT)), j)
            link(nc.vector.tensor_reduce(amax, aff, AX.X, ALU.max))
            say(tt(aff, aff, last(amax, NE2), ALU.subtract), "aff_max")
            dve.wait_ge(S("aff_exp"), 1)
            link(nc.vector.tensor_reduce(asum, aff, AX.X, ALU.add))
            link(nc.vector.reciprocal(asum, asum))
            say(tt(aff, aff, last(asum, NE2), ALU.mult), "aff_ready")
            is_out(dve, J("affT"))
            for r in range(CAP // 8):
                link(nc.vector.max(out=top8, in_=work))
                link(nc.vector.match_replace(out=work, in_to_replace=top8, in_values=work, imm_value=-1.0))
            link(ts(work, work, 0.0, None, ALU.is_lt))
            link(ts(affT, work, 0.0, 1.0, ALU.mult, ALU.add))
            link(nc.vector.tensor_tensor_scan(sel, affT, work, 0.0, ALU.mult, ALU.add))
            link(tt(sel, sel, work, ALU.mult))
            say(ts(sel, sel, -1.0, None, ALU.add), "rank_ready")
            j = J("rankT")
            is_full(dve, j)
            carried(cp(rank, v3(bank(j, 32), TT)), j)
            for t in range(TT):
                ins = tt(v3(onep[:, t, :], NE2), last(rank[:, t, :], CAP), mid(msk("slot"), NE2), ALU.is_equal)
            link(ins)
            for t in range(TT):
                ins = tt(v3(gatep[:, t, :], NE2), v3(onep[:, t, :], NE2), last(aff[:, t, :], CAP), ALU.mult)
            say(ins, "onehot_ready")
            say(nc.vector.memset(zrow, 0.0), "zeros2_ready")
            with dve.Fori(0, NE2 // 4) as i:
                for j in range(4):
                    dve.wait_ge(S("silu2_ready"), i * 4 + (j + 1))
                    tt(hid2, sg2, ps[64:128, (j % 2) * 512:(j % 2) * 512 + 512], ALU.mult).then_inc(S("hid2_ready"), 1)
                    dve.wait_ge(S("down2_tiles"), i * 8 + (2 * j + 2))
                    cp(YE[:, 512:1024], ps[:, 1536:2048]).then_inc(S("ye1_ready"), 1)
            dve.wait_ge(S("comb2_done"), 1)
            for t in range(TT):
                for half in range(2):
                    b = 4 + 2 * t + half
                    c = slice(half * 512, half * 512 + 512)
                    ins = tt(x[:, t, c], x[:, t, c], ps[:, b * 512:b * 512 + 512], ALU.add)
            link(ins)
            rms_norm(x, x, None)
            dve.wait_ge(S("fg_loaded"), 16)
            say(tt(x[:], x[:], mid(fg, TT), ALU.mult), "out_ready")


_SHAPES = {
    "x": (256, 1024), "ada_w": (1024, 6144), "w_in": (1024, 8728), "cmp_pos_k": (32, 128), "cmp_pos_v": (32, 128),
    "cmp_w1_k": (4096, 128), "cmp_w1_v": (4096, 128), "cmp_w2_k": (128, 128), "cmp_w2_v": (128, 128),
    "w_br_hg": (1024, 1024), "w_br_nsa": (1024, 1024), "w_out": (1024, 1024), "router_grp_w": (1024, 4),
    "router_exp_w": (1024, 32), "exp_w1": (32, 1024, 512), "exp_w3": (32, 1024, 512), "exp_w2": (32, 512, 1024),
    "mem_2": (256, 1024), "w_in_2": (1024, 2560), "w_mk_2": (1024, 256), "w_mv_2": (1024, 256),
    "conv_w_2": (31, 384), "shift_mu_2": (2, 1536), "decay_w0_2": (2, 384), "iclr_a0_2": (2, 384),
    "decay_up_2": (128, 384), "iclr_up_2": (128, 384), "gate_up_2": (128, 384), "r_k_2": (1, 384),
    "w_out_2": (1024, 1024), "w_router_2": (1024, 16), "w_e_gate_2": (16, 1024, 1024),
    "w_e_up_2": (16, 1024, 1024), "w_e_down_2": (16, 1024, 1024), "final_norm_g_2": (1, 1024),
}


def kernel(**inputs):
    import numpy as _np
    import concourse.bacc as _bacc
    from concourse import mybir as _mybir
    from concourse.bass_utils import run_bass_kernel_spmd as _run

    nc = _bacc.Bacc("TRN2", target_bir_lowering=False, num_devices=1)
    arrays, A = {}, {}
    fixed = {"cst": CST_A, "masks": MSK_A, "causal": causal(), "onehot": buckets()}
    for name, a in list(inputs.items()) + list(fixed.items()):
        a = _np.ascontiguousarray(a)
        if name in _SHAPES:
            a = a.reshape(_SHAPES[name])
        arrays[f"in_{name}"] = a
        A[name] = nc.dram_tensor(f"in_{name}", a.shape, _mybir.dt.from_np(a.dtype), kind="ExternalInput").ap()
    out = nc.dram_tensor("out_x", (T, D), F32, kind="ExternalOutput").ap()
    build(nc, A, out)
    r = _run(nc, [arrays], core_ids=[0])
    return r.results[0]["out_x"].reshape(1, T, D)
```
